# Optimizing a Trainium2 kernel written in Bass

```python
import math
import jax, jax.numpy as jnp
from jax import lax
import numpy as np

D_MODEL = 1024
BATCH = 1
SEQ = 256
DEPTH = 1
DEC_BATCH = 1
DEC_SEQ = 64
PAST_LEN = 128

CHUNK = 64
MIX_WIDTH = D_MODEL
SB_HEAD_DIM = 64
SB_WIDTH = MIX_WIDTH // 2
SB_HEADS = SB_WIDTH // SB_HEAD_DIM
ML_HEAD_DIM = 128
ML_WIDTH = MIX_WIDTH - SB_WIDTH
ML_HEADS = ML_WIDTH // ML_HEAD_DIM
CONV_W = 4
QBLK = 128
N_EXPERTS = 32
TOP_K = 4
D_FF = D_MODEL
SWIGLU_LIMIT = 7.0
SWIGLU_ALPHA = 1.702
MOE_BLK = 128
EPS = 1e-6
SPLITS = (SB_WIDTH, 2 * SB_WIDTH, 3 * SB_WIDTH, 3 * SB_WIDTH + 2 * ML_WIDTH,
          3 * SB_WIDTH + 3 * ML_WIDTH, 3 * SB_WIDTH + 3 * ML_WIDTH + 2 * ML_HEADS)
IN_COLS = 3 * SB_WIDTH + 4 * ML_WIDTH + 2 * ML_HEADS

kernel_name = "streaming_sb_mlstm_moe_adaln"

def rmsnorm(x, g):
    xf = x.astype(jnp.float32)
    y = xf * lax.rsqrt(jnp.mean(xf * xf, axis=-1, keepdims=True) + EPS)
    return (y * g.astype(jnp.float32)).astype(x.dtype)

def stick_breaking_attention(q, k, v, q_offset):
    sq = q.shape[1]
    scale = 1.0 / math.sqrt(q.shape[-1])
    outs = []
    for start in range(0, sq, QBLK):
        stop = min(start + QBLK, sq)
        kend = q_offset + stop
        qb = q[:, start:stop].astype(jnp.float32)
        kb = k[:, :kend].astype(jnp.float32)
        vb = v[:, :kend].astype(jnp.float32)
        z = jnp.einsum('bqhd,bkhd->bhqk', qb, kb) * scale
        qpos = q_offset + start + jnp.arange(stop - start)
        kpos = jnp.arange(kend)
        mask = kpos[None, :] < qpos[:, None]
        log_1m = jnp.where(mask, jax.nn.log_sigmoid(-z), 0.0)
        between = lax.cumsum(log_1m, axis=3, reverse=True) - log_1m
        a = jnp.where(mask, jnp.exp(jax.nn.log_sigmoid(z) + between), 0.0)
        outs.append(jnp.einsum('bhqk,bkhd->bqhd', a, vb))
    return jnp.concatenate(outs, axis=1).astype(q.dtype)

def mlstm_chunk(carry, inp):
    c_mat, n_vec, m_st = carry
    q, k, v, ig, lf = inp
    L = q.shape[1]
    b = jnp.cumsum(lf, axis=1)
    causal = jnp.tril(jnp.ones((L, L), dtype=bool))[None, :, :, None]
    d_log = jnp.where(causal, b[:, :, None, :] - b[:, None, :, :] + ig[:, None, :, :], -jnp.inf)
    inter = b + m_st[:, None, :]
    m_t = jnp.maximum(inter, jnp.max(d_log, axis=2))
    w_intra = jnp.exp(d_log - m_t[:, :, None, :])
    w_inter = jnp.exp(inter - m_t)
    s = jnp.einsum('bthd,bshd->btsh', q, k) * w_intra
    num = jnp.einsum('btsh,bshv->bthv', s, v) + w_inter[..., None] * jnp.einsum('bhvd,bthd->bthv', c_mat, q)
    den = jnp.sum(s, axis=2) + w_inter * jnp.einsum('bhd,bthd->bth', n_vec, q)
    h = num / jnp.maximum(jnp.abs(den), jnp.exp(-m_t))[..., None]
    b_last = b[:, -1]
    g = b_last[:, None, :] - b + ig
    m_new = jnp.maximum(b_last + m_st, jnp.max(g, axis=1))
    w_state = jnp.exp(g - m_new[:, None, :])
    decay = jnp.exp(b_last + m_st - m_new)
    c_new = decay[..., None, None] * c_mat + jnp.einsum('bsh,bshv,bshd->bhvd', w_state, v, k)
    n_new = decay[..., None] * n_vec + jnp.einsum('bsh,bshd->bhd', w_state, k)
    return (c_new, n_new, m_new), h

def mlstm(q, k, v, ig, lf, c0, n0, m0):
    bsz, s = q.shape[:2]
    L = min(CHUNK, s)
    nc = s // L

    def to_chunks(a):
        return jnp.swapaxes(a.reshape((bsz, nc, L) + a.shape[2:]), 0, 1)

    carry, h = lax.scan(mlstm_chunk, (c0, n0, m0),
                        (to_chunks(q), to_chunks(k), to_chunks(v), to_chunks(ig), to_chunks(lf)))
    h = jnp.swapaxes(h, 0, 1).reshape((bsz, s) + h.shape[3:])
    return h, carry

def causal_conv(u, past, w, b):
    full = jnp.concatenate([past.astype(u.dtype), u], axis=1)
    s = u.shape[1]
    y = b + full[:, 0:s] * w[0]
    for j in range(1, CONV_W):
        y = y + full[:, j:j + s] * w[j]
    return y, full[:, -(CONV_W - 1):]

def moe_ffn(h, w_router, b_router, w_gu, b_gu, w_down, b_down):
    t, d = h.shape
    logits = h.astype(jnp.float32) @ w_router.astype(jnp.float32) + b_router.astype(jnp.float32)
    top_val, top_idx = lax.top_k(logits, TOP_K)
    gates = jax.nn.softmax(top_val, axis=-1)
    tk = t * TOP_K
    flat_e = top_idx.reshape(-1).astype(jnp.int32)
    flat_tok = jnp.repeat(jnp.arange(t, dtype=jnp.int32), TOP_K)
    flat_gate = gates.reshape(-1)
    order = jnp.argsort(flat_e)
    se = flat_e[order]
    counts = jnp.bincount(flat_e, length=N_EXPERTS).astype(jnp.int32)
    padded = (counts + MOE_BLK - 1) // MOE_BLK * MOE_BLK
    pad_end = jnp.cumsum(padded)
    pad_start = pad_end - padded
    grp_start = jnp.cumsum(counts) - counts
    dest = pad_start[se] + jnp.arange(tk, dtype=jnp.int32) - grp_start[se]
    n_blocks = (tk + N_EXPERTS * (MOE_BLK - 1) + MOE_BLK - 1) // MOE_BLK
    n_rows = n_blocks * MOE_BLK
    row_tok = jnp.zeros((n_rows,), jnp.int32).at[dest].set(flat_tok[order])
    row_gate = jnp.zeros((n_rows,), jnp.float32).at[dest].set(flat_gate[order])
    block_exp = jnp.minimum(jnp.searchsorted(pad_end, jnp.arange(n_blocks, dtype=jnp.int32) * MOE_BLK, side='right'),
                            N_EXPERTS - 1)

    def step(acc, blk):
        tok, gate, e = blk
        xb = h[tok]
        gu = xb @ w_gu[e] + b_gu[e]
        x_glu, x_lin = jnp.split(gu, 2, axis=-1)
        x_glu = jnp.minimum(x_glu, SWIGLU_LIMIT)
        x_lin = jnp.clip(x_lin, -SWIGLU_LIMIT, SWIGLU_LIMIT)
        act = x_glu * jax.nn.sigmoid(SWIGLU_ALPHA * x_glu) * (x_lin + 1.0)
        out = (act @ w_down[e] + b_down[e]).astype(jnp.float32) * gate[:, None]
        return acc.at[tok].add(out), None

    acc, _ = lax.scan(step, jnp.zeros((t, d), jnp.float32),
                      (row_tok.reshape(n_blocks, MOE_BLK), row_gate.reshape(n_blocks, MOE_BLK), block_exp))
    return acc.astype(h.dtype)

def trunk_layer(x, c, k_past, v_past, conv_past, c0, n0, m0, w_ada, b_ada, g_norm1, w_in, g_q, g_k,
                w_conv, b_conv, b_gate, g_head, w_out, g_norm2, w_router, b_router, w_gu, b_gu, w_down, b_down):
    bsz, s, d = x.shape
    past = k_past.shape[1]
    mod = jax.nn.silu(c) @ w_ada + b_ada
    sh1, sc1, ga1, sh2, sc2, ga2 = [m[:, None, :] for m in jnp.split(mod, 6, axis=-1)]
    h = rmsnorm(x, g_norm1) * (1.0 + sc1) + sh1
    u = h @ w_in
    sb_q, sb_k, sb_v, ml_qk, ml_v, ml_gate, ml_o = jnp.split(u, SPLITS, axis=-1)
    q = rmsnorm(sb_q.reshape(bsz, s, SB_HEADS, SB_HEAD_DIM), g_q)
    k = rmsnorm(sb_k.reshape(bsz, s, SB_HEADS, SB_HEAD_DIM), g_k)
    v = sb_v.reshape(bsz, s, SB_HEADS, SB_HEAD_DIM)
    k_all = jnp.concatenate([k_past.astype(k.dtype), k], axis=1)
    v_all = jnp.concatenate([v_past.astype(v.dtype), v], axis=1)
    o_sb = stick_breaking_attention(q, k_all, v_all, past).reshape(bsz, s, SB_WIDTH)
    qk_c, conv_new = causal_conv(ml_qk, conv_past, w_conv, b_conv)
    mq, mk = jnp.split(jax.nn.silu(qk_c).astype(jnp.float32), 2, axis=-1)
    mq = mq.reshape(bsz, s, ML_HEADS, ML_HEAD_DIM)
    mk = mk.reshape(bsz, s, ML_HEADS, ML_HEAD_DIM) * (ML_HEAD_DIM ** -0.5)
    mv = ml_v.astype(jnp.float32).reshape(bsz, s, ML_HEADS, ML_HEAD_DIM)
    ig, fg = jnp.split(ml_gate.astype(jnp.float32) + b_gate.astype(jnp.float32), 2, axis=-1)
    h_ml, (c_new, n_new, m_new) = mlstm(mq, mk, mv, ig, jax.nn.log_sigmoid(fg),
                                        c0.astype(jnp.float32), n0.astype(jnp.float32), m0.astype(jnp.float32))
    h_ml = rmsnorm(h_ml, g_head).reshape(bsz, s, ML_WIDTH).astype(x.dtype)
    o_ml = jax.nn.sigmoid(ml_o) * h_ml
    mix = jnp.concatenate([o_sb, o_ml], axis=-1) @ w_out
    x = x + ga1 * mix
    h2 = rmsnorm(x, g_norm2) * (1.0 + sc2) + sh2
    ff = moe_ffn(h2.reshape(bsz * s, d), w_router, b_router, w_gu, b_gu, w_down, b_down).reshape(bsz, s, d)
    x = x + ga2 * ff
    return x, k, v, conv_new, c_new, n_new, m_new

def setup_inputs(seed: int = 0) -> dict:
    key = jax.random.key(seed)
    ks = jax.random.split(key, 32)
    f32 = jnp.float32

    def nrm(k, shape, scale):
        return jax.random.normal(k, shape, f32) * scale

    b_gate = jnp.concatenate([nrm(ks[14], (DEPTH, ML_HEADS), 0.1),
                              jnp.linspace(3.0, 6.0, ML_HEADS, dtype=f32)[None, :] + nrm(ks[15], (DEPTH, ML_HEADS), 0.1)],
                             axis=-1)
    return {
        "x_prompt": nrm(ks[0], (BATCH, SEQ, D_MODEL), 1.0),
        "x_sample": nrm(ks[1], (DEC_BATCH, DEC_SEQ, D_MODEL), 1.0),
        "c_prompt": nrm(ks[2], (BATCH, D_MODEL), 1.0),
        "c_sample": nrm(ks[3], (DEC_BATCH, D_MODEL), 1.0),
        "cache_sb_k": nrm(ks[4], (DEPTH, DEC_BATCH, PAST_LEN, SB_HEADS, SB_HEAD_DIM), 1.0),
        "cache_sb_v": nrm(ks[5], (DEPTH, DEC_BATCH, PAST_LEN, SB_HEADS, SB_HEAD_DIM), 1.0),
        "state_conv": nrm(ks[6], (DEPTH, DEC_BATCH, CONV_W - 1, 2 * ML_WIDTH), 1.0),
        "state_mlstm_c": nrm(ks[7], (DEPTH, DEC_BATCH, ML_HEADS, ML_HEAD_DIM, ML_HEAD_DIM), 0.1),
        "state_mlstm_n": nrm(ks[8], (DEPTH, DEC_BATCH, ML_HEADS, ML_HEAD_DIM), 0.1),
        "state_mlstm_m": nrm(ks[9], (DEPTH, DEC_BATCH, ML_HEADS), 1.0),
        "w_ada": nrm(ks[10], (DEPTH, D_MODEL, 6 * D_MODEL), 0.5 * D_MODEL ** -0.5),
        "b_ada": nrm(ks[11], (DEPTH, 6 * D_MODEL), 0.02),
        "g_norm1": 1.0 + nrm(ks[12], (DEPTH, D_MODEL), 0.05),
        "w_in": nrm(ks[13], (DEPTH, D_MODEL, IN_COLS), D_MODEL ** -0.5),
        "g_q": 1.0 + nrm(ks[16], (DEPTH, SB_HEAD_DIM), 0.05),
        "g_k": 1.0 + nrm(ks[17], (DEPTH, SB_HEAD_DIM), 0.05),
        "w_conv": nrm(ks[18], (DEPTH, CONV_W, 2 * ML_WIDTH), CONV_W ** -0.5),
        "b_conv": nrm(ks[19], (DEPTH, 2 * ML_WIDTH), 0.02),
        "b_gate": b_gate,
        "g_head": 1.0 + nrm(ks[20], (DEPTH, ML_HEAD_DIM), 0.05),
        "w_out": nrm(ks[21], (DEPTH, MIX_WIDTH, D_MODEL), MIX_WIDTH ** -0.5),
        "g_norm2": 1.0 + nrm(ks[22], (DEPTH, D_MODEL), 0.05),
        "w_router": nrm(ks[23], (DEPTH, D_MODEL, N_EXPERTS), D_MODEL ** -0.5),
        "b_router": nrm(ks[24], (DEPTH, N_EXPERTS), 0.01),
        "w_gu": nrm(ks[25], (DEPTH, N_EXPERTS, D_MODEL, 2 * D_FF), D_MODEL ** -0.5),
        "b_gu": nrm(ks[26], (DEPTH, N_EXPERTS, 2 * D_FF), 0.02),
        "w_down": nrm(ks[27], (DEPTH, N_EXPERTS, D_FF, D_MODEL), D_FF ** -0.5),
        "b_down": nrm(ks[28], (DEPTH, N_EXPERTS, D_MODEL), 0.02),
    }

def reference(x_prompt, x_sample, c_prompt, c_sample, cache_sb_k, cache_sb_v, state_conv, state_mlstm_c,
              state_mlstm_n, state_mlstm_m, w_ada, b_ada, g_norm1, w_in, g_q, g_k, w_conv, b_conv, b_gate,
              g_head, w_out, g_norm2, w_router, b_router, w_gu, b_gu, w_down, b_down):
    bsz = x_prompt.shape[0]
    dt = x_prompt.dtype
    kv0 = jnp.zeros((bsz, 0, SB_HEADS, SB_HEAD_DIM), dt)
    conv0 = jnp.zeros((bsz, CONV_W - 1, 2 * ML_WIDTH), dt)
    c0 = jnp.zeros((bsz, ML_HEADS, ML_HEAD_DIM, ML_HEAD_DIM), jnp.float32)
    n0 = jnp.zeros((bsz, ML_HEADS, ML_HEAD_DIM), jnp.float32)
    m0 = jnp.zeros((bsz, ML_HEADS), jnp.float32)
    yp, ys = x_prompt, x_sample
    sp = [[] for _ in range(6)]
    ss = [[] for _ in range(6)]
    for l in range(DEPTH):
        yp, *st_p = trunk_layer(yp, c_prompt, kv0, kv0, conv0, c0, n0, m0, w_ada[l], b_ada[l], g_norm1[l],
                                w_in[l], g_q[l], g_k[l], w_conv[l], b_conv[l], b_gate[l], g_head[l], w_out[l],
                                g_norm2[l], w_router[l], b_router[l], w_gu[l], b_gu[l], w_down[l], b_down[l])
        ys, *st_s = trunk_layer(ys, c_sample, cache_sb_k[l], cache_sb_v[l], state_conv[l], state_mlstm_c[l],
                                state_mlstm_n[l], state_mlstm_m[l], w_ada[l], b_ada[l], g_norm1[l],
                                w_in[l], g_q[l], g_k[l], w_conv[l], b_conv[l], b_gate[l], g_head[l], w_out[l],
                                g_norm2[l], w_router[l], b_router[l], w_gu[l], b_gu[l], w_down[l], b_down[l])
        for i in range(6):
            sp[i].append(st_p[i])
            ss[i].append(st_s[i])
    kp, vp, convp, cp, np_, mp = [jnp.stack(a, axis=0) for a in sp]
    ks_, vs, convs, cs, ns, ms = [jnp.stack(a, axis=0) for a in ss]
    return (yp, ys, kp, vp, convp, cp, np_, mp, ks_, vs, convs, cs, ns, ms)


_drawn_inputs = setup_inputs


def setup_inputs(seed=0):
    import zlib

    import numpy as np

    out = dict(_drawn_inputs(seed))
    spreads = {}
    factors = {'cache_sb_k': 6.605,
     'cache_sb_v': 3.406,
     'state_mlstm_n': 12.797,
     'state_mlstm_m': 2.836,
     'g_q': 16.02,
     'g_head': 5.077,
     'b_router': 4.576,
     'b_gu': 8.0,
     'b_down': 8.0}
    for name, (base, spread) in spreads.items():
        noise = np.random.default_rng([zlib.crc32(name.encode()), seed]).standard_normal(out[name].shape)
        drawn = base * np.exp(spread * noise) if base else spread * noise
        out[name] = __import__('jax').numpy.asarray(drawn.astype(out[name].dtype))
    for name, factor in factors.items():
        out[name] = (out[name] * factor).astype(out[name].dtype)
    return out
```

```python
from contextlib import ExitStack

import numpy as np
import concourse.bass as bass
from concourse import mybir

ALU = mybir.AluOpType
ACT = mybir.ActivationFunctionType
AX_X = mybir.AxisListType.X
F32 = mybir.dt.float32
BF16 = mybir.dt.bfloat16
U32 = mybir.dt.uint32
I32 = mybir.dt.int32

P = 128
D = 1024
KD = D // P
TP, TS = 256, 64
T = TP + TS
TILES = ((0, 128), (128, 128), (256, 64))
PAST = 128
SBH, SBD = 8, 64
MLH, MLD = 4, 128
CW = 4
RAWW = CW - 1 + TP + CW - 1 + TS
CONVW = RAWW - (CW - 1)
CS = TP + CW - 1
NE, TOPK = 32, 4
CAP = 96
SWIGLU_LIMIT, SWIGLU_ALPHA = 7.0, 1.702

CHC = 256
SLOTS = 12
ADA1, SBP, MLP, ADA2, WO = 8, 6, 8, 16, 4
PRE = ADA1 + SBP + MLP + ADA2 + WO
S0 = PRE % SLOTS
PASSES = -(-T // CAP)

A, C, B, E, DP = slice(0, 128), slice(128, 256), slice(256, 384), slice(384, 448), slice(448, 512)
AC, BE, ACBE = slice(0, 256), slice(256, 448), slice(0, 448)

SMALL = {}
_at = 0
for _n, _w in (("g1", 8), ("g2", 8), ("b_ada", 48), ("b_conv", 8), ("w_conv", 8 * CW), ("gq", 1), ("gk", 1), ("gh", 1),
               ("n0", MLH), ("cT", 16), ("m0b", MLH), ("b_router", NE), ("eps", 1), ("conv_past", 8 * 3),
               ("bgate", 2), ("m0c", 1), ("w_router", KD * NE)):
    SMALL[_n] = (_at, _at + _w)
    _at += _w
NSMALL = _at
CONST = {}
_at = 0
for _n, _w in (("ident", P), ("ones", P), ("tri", P), ("blk", P), ("mask_s", 448), ("mask_i", 448), ("sel", MLH * P),
               ("iota_e", NE), ("iota_c", CAP)):
    CONST[_n] = (_at, _at + _w)
    _at += _w
NCONST = _at


class Chain:

    def __init__(self, eng, sem):
        self.eng, self.sem, self.n = eng, sem, 0

    def step(self, ins):
        ins.then_inc(self.sem, 1)
        self.n = self.n + 1

    def wait(self):
        self.eng.wait_ge(self.sem, self.n)

    def __call__(self, ins):
        self.step(ins)
        self.wait()


def build(nc, xT, small, const, b_gu, b_down, kcT, vc, c0, c0T, w_ada, w_in, w_out, w_gu, w_down,
          yT, koT, voT, convo, co, no, mo):
    ctx = ExitStack()
    with ctx:
        def sb(name, shape, dt=F32):
            return ctx.enter_context(nc.sbuf_tensor(name, shape, dt))

        def sem(name):
            return ctx.enter_context(nc.semaphore(name))

        ring = sb("ring", [P, SLOTS, 8, CHC])
        csb = sb("csb", [P, NCONST])
        ssb = sb("ssb", [P, NSMALL])
        x = sb("x", [P, KD, T])
        h = sb("h", [P, KD, T])
        wgate = sb("wgate", [P, KD, 8])
        tiny = sb("tiny", [P, 400])
        WORK = 18760
        work = sb("work", [P, WORK])
        bank = [ctx.enter_context(nc.psum_tensor(f"bank{i}", [P, 512], F32)) for i in range(8)]

        def K(name):
            return csb[:, CONST[name][0]:CONST[name][1]]

        def Sm(name):
            return ssb[:, SMALL[name][0]:SMALL[name][1]]

        ident, ones, tri, blk = K("ident"), K("ones"), K("tri"), K("blk")
        mask_s, mask_i, iota_e, iota_c = K("mask_s"), K("mask_i"), K("iota_e"), K("iota_c")
        sel = K("sel").rearrange("p (h n) -> p h n", h=MLH)
        wrout = Sm("w_router").rearrange("p (k e) -> p k e", k=KD)
        eps = Sm("eps")

        def region(start):
            at = [start]

            def take(*dims, dt=F32):
                n = int(np.prod(dims))
                cols = n if dt == F32 else n // 2
                v = work[:, at[0]:at[0] + cols]
                at[0] += cols
                assert at[0] <= WORK, at[0]
                if dt != F32:
                    v = v.bitcast(dt)
                if len(dims) > 1:
                    names = "abcd"[:len(dims)]
                    v = v.rearrange(f"p ({' '.join(names)}) -> p {' '.join(names)}", **dict(zip(names, dims)))
                return v
            return take, at

        take, at = region(0)
        q = take(4, T)
        k = take(4, 384)
        vT = take(4, T)
        kc = take(4, PAST)
        vpast = take(512)
        vtok = take(3, 512)
        end_sb = at[0]
        raw = take(8, RAWW)
        y = take(8, CONVW)
        mo_g = take(4, T)
        mix = take(8, T)
        mvT = mix[:, 4:8, :]
        scr = take(6, 512)
        take2, at2 = region(0)
        mq = take2(4, T)
        mk = take2(4, 384)
        mvtok = take2(3, 512)
        mktok = take2(3, 512)
        assert at2[0] <= end_sb
        sgy = raw.rearrange("p a b -> p (a b)")[:, 0:8 * CONVW].rearrange("p (a b) -> p a b", a=8)
        take3, at3 = region(end_sb + 8 * RAWW)
        C0 = take3(MLH, P)
        C0T = take3(MLH, P)
        Cout = take3(2, MLH, P)
        hh = take3(T)
        assert at3[0] <= end_sb + 8 * RAWW + 8 * CONVW
        sq = mix
        take4, _ = region(0)
        h2p = take4(3, 3, D, dt=BF16)
        xg = take4(KD, CAP)
        act = take4(8, CAP)
        ub = take4(4, CAP)
        gc = take4(2, CAP)
        lc = take4(2, CAP)
        sg = take4(2, CAP)
        oT = take4(8, CAP)
        otok = take4(D)
        spread = take4(T)
        pick = take4(3, CAP, dt=BF16)
        wpick = take4(3, CAP)
        acc = take4(8, T)
        res = take4(2, 512)
        member = take4(3, NE)
        gate = take4(3, NE)
        rank = take4(3, NE)
        lg = take4(3, NE)
        bgu = take4(NE, 16)
        bdn = take4(NE, 8)

        tat = [0]

        def tn(*dims, dt=F32):
            n = int(np.prod(dims))
            v = tiny[:, tat[0]:tat[0] + n]
            tat[0] += n
            if dt != F32:
                v = v.bitcast(dt)
            if len(dims) > 1:
                names = "abcd"[:len(dims)]
                v = v.rearrange(f"p ({' '.join(names)}) -> p {' '.join(names)}", **dict(zip(names, dims)))
            return v

        cs = tn(KD, 2)
        mod = tn(48, 2)
        s1 = tn(KD, 2)
        s2 = tn(KD, 2)
        gqs = tn(1)
        gtok = tn(3, 8)
        acol = tn(3, MLH)
        nout = tn(2, MLH)
        mout = tn(2)
        top = tn(3, 8)
        topi = tn(3, 8, dt=U32)
        topf = tn(3, 8)
        negv = tn(3)
        rs4 = tn(3)
        cnt = tn(NE)
        cmax = tn(1)
        cmaxi = tn(1, dt=I32)
        rows = sb("rows", [P, 4, T])

        ld_small = sem("ld_small")
        ld_side = sem("ld_side")
        ld_bias = sem("ld_bias")
        ld_state = sem("ld_state")
        slot_full = [sem(f"slot_full{i}") for i in range(SLOTS)]
        v_chain, a_chain, g_chain = sem("v_chain"), sem("a_chain"), sem("g_chain")
        v_init = sem("v_init")
        csig = sem("csig")
        cs_ready = sem("cs_ready")
        xsq_ready = sem("xsq_ready")
        ss1_ps = sem("ss1_ps")
        rstd1_ready = sem("rstd1_ready")
        hs_ready = sem("hs_ready")
        h_ready = sem("h_ready")
        ada_used = sem("ada_used")
        mod1_ready = sem("mod1_ready")
        mod2_ready = sem("mod2_ready")
        proj_ps = sem("proj_ps")
        sq_ready = sem("sq_ready")
        proj_done = sem("proj_done")
        nss_ps = sem("nss_ps")
        nrs_ready = sem("nrs_ready")
        qk_ready = sem("qk_ready")
        vtr_ps = sem("vtr_ps")
        vtok_ready = sem("vtok_ready")
        gates_ps = sem("gates_ps")
        gtok_ready = sem("gtok_ready")
        grow_ps = sem("grow_ps")
        frow_ready = sem("frow_ready")
        flog_ready = sem("flog_ready")
        rows_ready = sem("rows_ready")
        conv_ready = sem("conv_ready")
        z_ps = sem("z_ps")
        l_ready = sem("l_ready")
        sp_ready = sem("sp_ready")
        spm_ready = sem("spm_ready")
        between_ps = sem("between_ps")
        t_ready = sem("t_ready")
        e_ready = sem("e_ready")
        a_ready = sem("a_ready")
        av_ps = sem("av_ps")
        av_done = sem("av_done")
        sgy_ready = sem("sgy_ready")
        mkq_ready = sem("mkq_ready")
        ktr_ps = sem("ktr_ps")
        mvtr_ps = sem("mvtr_ps")
        ktok_ready = sem("ktok_ready")
        mvtok_ready = sem("mvtok_ready")
        acol_ps = sem("acol_ps")
        acol_ready = sem("acol_ready")
        mb_ps = sem("mb_ps")
        mt_ps = sem("mt_ps")
        st_ps = sem("st_ps")
        wtmp_ready = sem("wtmp_ready")
        w_ready = sem("w_ready")
        s_ready = sem("s_ready")
        sm_ready = sem("sm_ready")
        qw_ready = sem("qw_ready")
        kw_ready = sem("kw_ready")
        num_ps = sem("num_ps")
        state_ps = sem("state_ps")
        hd_ready = sem("hd_ready")
        hsq_ready = sem("hsq_ready")
        hss_ps = sem("hss_ps")
        hrs_ready = sem("hrs_ready")
        mix_ready = sem("mix_ready")
        state_out = sem("state_out")
        xo_ps = sem("xo_ps")
        x1_ready = sem("x1_ready")
        x1sq_ready = sem("x1sq_ready")
        ss2_ps = sem("ss2_ps")
        rstd2_ready = sem("rstd2_ready")
        hs2_ready = sem("hs2_ready")
        h2_ready = sem("h2_ready")
        logit_ps = sem("logit_ps")
        top_ready = sem("top_ready")
        ex_ready = sem("ex_ready")
        member_ready = sem("member_ready")
        rank_ps = sem("rank_ps")
        cnt_ready = sem("cnt_ready")
        h2tr_ps = sem("h2tr_ps")
        hi_ready = sem("hi_ready")
        r_ready = sem("r_ready")
        mid_ready = sem("mid_ready")
        lo_ready = sem("lo_ready")
        rank_moved = sem("rank_moved")
        pick_ready = sem("pick_ready")
        gath_ps = sem("gath_ps")
        xg_ready = sem("xg_ready")
        glu_used = sem("glu_used")
        gu_ps = sem("gu_ps")
        u_ready = sem("u_ready")
        gc_ready = sem("gc_ready")
        lc_ready = sem("lc_ready")
        sg_ready = sem("sg_ready")
        gl_ready = sem("gl_ready")
        act_ready = sem("act_ready")
        dn_used = sem("dn_used")
        dn_ps = sem("dn_ps")
        dn_ready = sem("dn_ready")
        wpick_ready = sem("wpick_ready")
        otr_ps = sem("otr_ps")
        otok_ready = sem("otok_ready")
        str_ps = sem("str_ps")
        spread_ready = sem("spread_ready")
        sc_ps = sem("sc_ps")
        acc_ready = sem("acc_ready")
        acc_closed = sem("acc_closed")
        y_ready = sem("y_ready")
        sb_stored = sem("sb_stored")
        conv_stored = sem("conv_stored")
        state_stored = sem("state_stored")
        y_stored = sem("y_stored")

        def tok(tt):
            return slice(TILES[tt][0], TILES[tt][0] + TILES[tt][1])

        SEQ = ((slice(0, TP), 0), (slice(TP, T), 1))

        def expert_chunks(e):
            gu = w_gu.rearrange("o e (k p) n -> (o e) p k n", p=P)
            dn = w_down.rearrange("o e (k p) n -> (o e) p k n", p=P)
            out = []
            for j in range(4):
                out.append(gu[e, :, :, j * CHC:(j + 1) * CHC])
                out.append(gu[e, :, :, D + j * CHC:D + (j + 1) * CHC])
            for j in range(4):
                out.append(dn[e, :, :, j * CHC:(j + 1) * CHC])
            return out

        def expert_turn(j):
            return (S0 + j) % SLOTS, (PRE + j) // SLOTS

        def used_before(n):
            if n < ADA1:
                return ada_used, n + 1
            n -= ADA1
            if n < SBP + MLP:
                return proj_ps, 2 * n + 2
            n -= SBP + MLP
            if n < ADA2:
                return ada_used, ADA1 + n + 1
            return xo_ps, 2 * (n - ADA2) + 2

        def used_expert(j, turn):
            if j < 8:
                return (gu_ps if j % 2 else glu_used), turn * 4 + (j // 2 + 1)
            return (dn_ps if j % 2 else dn_used), turn * 2 + ((j - 8) // 2 + 1)

        def passes(eng, start, expert, finish):
            start(0, 0, 0)
            expert(0, 0, True, True, False)
            with eng.Fori(1, NE - 1) as e:
                expert(e, e, False, False, False)
            expert(NE - 1, NE - 1, False, False, True)
            finish(NE - 1)
            eng.wait_ge(cnt_ready, 1)
            most = eng.value_load(cmaxi[0:1, 0:1], min_val=0, max_val=T)
            with eng.Fori(1, PASSES) as b:
                with eng.If(most > b * CAP):
                    start(b * NE, 0, b)
                    expert(b * NE, 0, False, True, False)
                    with eng.Fori(1, NE - 1) as e:
                        expert(b * NE + e, e, False, False, False)
                    expert(b * NE + (NE - 1), NE - 1, False, False, True)
                    finish(b * NE + (NE - 1))

        block = ctx.enter_context(nc.Block())

        @block.sync
        def _(sp):
            ada = w_ada.rearrange("o (k p) n -> (o p) k n", p=P)
            win = w_in.rearrange("o (k p) n -> (o p) k n", p=P)
            wo = w_out.rearrange("o (k p) n -> (o p) k n", p=P)
            pre = [ada[:, :, j * CHC:(j + 1) * CHC] for j in range(ADA1)]
            pre += [win[:, :, j * CHC:(j + 1) * CHC] for j in range(SBP + 6)]
            pre += [win[:, :, 3080 + j * CHC:3080 + (j + 1) * CHC] for j in range(2)]
            pre += [ada[:, :, j * CHC:(j + 1) * CHC] for j in range(ADA1, 24)]
            pre += [wo[:, :, j * CHC:(j + 1) * CHC] for j in range(WO)]
            assert len(pre) == PRE
            for n, src in enumerate(pre):
                if n >= SLOTS:
                    sp.wait_ge(*used_before(n - SLOTS))
                sp.dma_start(ring[:, n % SLOTS], src).then_inc(slot_full[n % SLOTS], 16)

            for j, src in enumerate(expert_chunks(0)):
                sp.wait_ge(*used_before(PRE + j - SLOTS))
                sp.dma_start(ring[:, expert_turn(j)[0]], src).then_inc(slot_full[expert_turn(j)[0]], 16)

            def load_expert(e, turn):
                for j, src in enumerate(expert_chunks(e)):
                    sp.wait_ge(*used_expert(j, turn - 1))
                    sp.dma_start(ring[:, expert_turn(j)[0]], src).then_inc(slot_full[expert_turn(j)[0]], 16)

            with sp.Fori(1, NE) as e:
                load_expert(e, e)
            sp.wait_ge(cnt_ready, 1)
            most = sp.value_load(cmaxi[0:1, 0:1], min_val=0, max_val=T)
            with sp.Fori(1, PASSES) as b:
                with sp.If(most > b * CAP):
                    with sp.Fori(0, NE) as e:
                        load_expert(e, b * NE + e)
            yv = yT.rearrange("(k p) t -> p k t", p=P)
            for c in range(4):
                sp.wait_ge(y_ready, 4 * (c + 1))
                sp.dma_start(yv[:, 2 * c:2 * c + 2, :], h[:, 2 * c:2 * c + 2, :]).then_inc(y_stored, 16)
            sp.wait_ge(y_stored, 16 * 4)
            sp.wait_ge(sb_stored, 16 * 2)
            sp.wait_ge(conv_stored, 16 * 2)
            sp.wait_ge(state_stored, 16 * 3)

        @block.tensor
        def _(pe):
            mm = nc.tensor.matmul
            used = [0]

            def chunk():
                n = used[0]
                pe.wait_ge(slot_full[n % SLOTS], 16 * (n // SLOTS + 1))
                used[0] += 1
                return ring[:, n % SLOTS]

            pe.wait_ge(ld_small, 16 * 4)
            pe.wait_ge(xsq_ready, 1)
            for kk in range(KD):
                last = mm(bank[7][:, 0:T], ones, sq[:, kk, :], start=kk == 0, stop=kk == KD - 1)
            last.then_inc(ss1_ps, 1)
            pe.wait_ge(cs_ready, 1)

            def ada_tiles(n, dst, first):
                for c in range(n):
                    w = chunk()
                    for i in range(2):
                        t = 2 * (first + c) + i
                        for kk in range(KD):
                            last = mm(dst(t), w[:, kk, i * P:(i + 1) * P], cs[:, kk, :], start=kk == 0, stop=kk == KD - 1)
                    last.then_inc(ada_used, 1)

            ada_tiles(ADA1, lambda t: bank[2][:, 2 * t:2 * t + 2], 0)
            pe.wait_ge(h_ready, 16)
            tile = [0]
            hold = [None]

            def proj():
                t = tile[0]
                if t % 2 == 0:
                    hold[0] = chunk()
                w = hold[0]
                if t >= 2:
                    pe.wait_ge(*((sq_ready, t - 1) if t < 10 else (proj_done, t - 9)))
                for kk in range(KD):
                    last = mm(bank[t % 2][:, 0:T], w[:, kk, (t % 2) * P:(t % 2 + 1) * P], h[:, kk, :], start=kk == 0, stop=kk == KD - 1)
                last.then_inc(proj_ps, 1)
                tile[0] += 1

            def nss(i):
                if i >= 2:
                    pe.wait_ge(nrs_ready, i - 1)
                pe.wait_ge(sq_ready, i + 1)
                mm(bank[6 + i % 2][:, 0:T], blk, scr[:, i % 2, 0:T], start=True, stop=True).then_inc(nss_ps, 1)

            for t in range(8):
                proj()
                if t >= 1:
                    nss(t - 1)
            proj()
            nss(7)
            for t in range(3):
                proj()
            for tt, (t0, n) in enumerate(TILES):
                for kk in range(KD):
                    last = mm(bank[5][0:n, tt * 8:tt * 8 + 8], h[:, kk, t0:t0 + n], wgate[:, kk, :], start=kk == 0, stop=kk == KD - 1)
            last.then_inc(gates_ps, 1)
            pe.wait_ge(proj_done, 4)
            pe.wait_ge(mod1_ready, 1)
            for tt, (t0, n) in enumerate(TILES):
                for c in range(4):
                    last = nc.tensor.transpose(bank[2 + tt][0:n, c * P:(c + 1) * P], vT[:, c, t0:t0 + n], ident)
                last.then_inc(vtr_ps, 1)
            pe.wait_ge(gtok_ready, 1)
            pe.wait_ge(nrs_ready, 8)
            for g in range(2):
                for tt, (t0, n) in enumerate(TILES):
                    last = nc.tensor.transpose(bank[6 + g][0:MLH, t0:t0 + n], gtok[0:n, tt, g * MLH:(g + 1) * MLH], ident[0:n, 0:n])
            last.then_inc(grow_ps, 1)
            pe.wait_ge(qk_ready, 8)
            pe.wait_ge(vtok_ready, 3)
            pe.wait_ge(ld_side, 16 * 2)

            def z_of(hd):
                r0 = 64 * (hd % 2)
                r = slice(r0, r0 + 64)
                c = hd // 2
                zb = bank[2 + hd % 2]
                if hd >= 2:
                    pe.wait_ge(t_ready, hd - 1)
                mm(zb[:, AC], k[r, c, 0:128], q[r, c, 0:256], start=True, stop=True)
                mm(zb[:, B], k[r, c, 128:256], q[r, c, 128:256], start=True, stop=True)
                mm(zb[:, E], k[r, c, 256:384], q[r, c, 256:320], start=True, stop=True)
                mm(zb[:, DP], kc[r, c, :], q[r, c, 256:320], start=True, stop=True).then_inc(z_ps, 1)

            def between_of(hd):
                pe.wait_ge(spm_ready, hd + 1)
                if hd >= 2:
                    pe.wait_ge(t_ready, hd - 1)
                sp_ = scr[:, 3 * (hd % 2) + 1, :]
                bb = bank[4 + hd % 2]
                mm(bb[:, :], tri, sp_, start=True, stop=False)
                mm(bb[:, C], ones, sp_[:, B], start=False, stop=False)
                mm(bb[:, DP], ones, sp_[:, E], start=False, stop=True).then_inc(between_ps, 1)

            def av_of(hd):
                pe.wait_ge(a_ready, hd + 1)
                if hd % 2 == 0 and hd:
                    pe.wait_ge(av_done, hd // 2)
                if hd == 0:
                    pe.wait_ge(frow_ready, 1)
                r = slice(64 * (hd % 2), 64 * (hd % 2) + 64)
                vc_ = slice(hd * 64, hd * 64 + 64)
                a_ = scr[:, 3 * (hd % 2) + 2, :]
                ob = bank[6]
                mm(ob[r, 0:128], vtok[:, 0, vc_], a_[:, A], start=True, stop=True)
                mm(ob[r, 128:256], vtok[:, 0, vc_], a_[:, C], start=True, stop=False)
                mm(ob[r, 128:256], vtok[:, 1, vc_], a_[:, B], start=False, stop=True)
                mm(ob[r, 256:320], vpast[:, vc_], a_[:, DP], start=True, stop=False)
                mm(ob[r, 256:320], vtok[0:64, 2, vc_], a_[0:64, E], start=False, stop=True).then_inc(av_ps, 1)

            for i in range(SBH + 2):
                if 1 <= i < SBH + 1:
                    between_of(i - 1)
                if i >= 2:
                    av_of(i - 2)
                if i < SBH:
                    z_of(i)
                    proj()
                    proj()

            pe.wait_ge(mkq_ready, 1)
            pe.wait_ge(proj_done, 20)
            pe.wait_ge(t_ready, 8)
            pe.wait_ge(av_done, 4)
            for tt, (t0, n) in enumerate(TILES):
                for c in range(4):
                    last = nc.tensor.transpose(bank[tt][0:n, c * P:(c + 1) * P], mk[:, c, t0:t0 + n], ident)
                last.then_inc(ktr_ps, 1)
            for tt, (t0, n) in enumerate(TILES):
                for c in range(4):
                    last = nc.tensor.transpose(bank[3 + tt][0:n, c * P:(c + 1) * P], mvT[:, c, t0:t0 + n], ident)
                last.then_inc(mvtr_ps, 1)
            pe.wait_ge(rows_ready, 1)
            for tt, (t0, n) in enumerate(TILES):
                last = nc.tensor.transpose(bank[6][0:n, tt * 4:tt * 4 + 4], rows[0:MLH, 0, t0:t0 + n], ident[0:MLH, 0:MLH])
            last.then_inc(acol_ps, 1)
            pe.wait_ge(ktok_ready, 3)
            pe.wait_ge(mvtok_ready, 3)
            pe.wait_ge(acol_ready, 1)
            pe.wait_ge(ld_state, 16 * 2)

            def ml_scores(i):
                if i:
                    pe.wait_ge(w_ready, i)
                mm_ = mm(bank[3][:, 0:T], sel[0:MLH, i, :], rows[0:MLH, 1, :], start=True, stop=True)
                mm_.then_inc(mb_ps, 1)
                mm(bank[4][:, 0:T], sel[0:MLH, i, :], rows[0:MLH, 3, :], start=True, stop=True).then_inc(mt_ps, 1)
                if i:
                    pe.wait_ge(s_ready, i)
                mm(bank[2][:, AC], mk[:, i, 0:128], mq[:, i, 0:256], start=True, stop=True)
                mm(bank[2][:, B], mk[:, i, 128:256], mq[:, i, 128:256], start=True, stop=True)
                mm(bank[2][:, E], mk[:, i, 256:384], mq[:, i, 256:320], start=True, stop=True).then_inc(st_ps, 1)

            def ml_values(i):
                S_ = scr[:, 1, :]
                qw = scr[:, 3, 0:64]
                nb = scr[:, 3, 64:192]
                kw = scr[:, 2, 0:384].rearrange("p (a b) -> p a b", a=3)
                pe.wait_ge(sm_ready, i + 1)
                pe.wait_ge(qw_ready, i + 1)
                hc = slice(i * P, (i + 1) * P)
                if i:
                    pe.wait_ge(hd_ready, i)
                for bk, l0, l1, l2, li in ((5, mvtok[:, 0, hc], mvtok[:, 1, hc], mvtok[0:64, 2, hc], C0T[:, i, :]),
                                           (6, ones, ones, ones[0:64, :], nb)):
                    mm(bank[bk][:, 0:256], l0, S_[:, AC], start=True, stop=False)
                    mm(bank[bk][:, 128:256], l1, S_[:, B], start=False, stop=True)
                    mm(bank[bk][:, 256:320], l2, S_[0:64, E], start=True, stop=False)
                    last = mm(bank[bk][:, 256:320], li, qw, start=False, stop=True)
                last.then_inc(num_ps, 1)
                pe.wait_ge(kw_ready, i + 1)
                if i:
                    pe.wait_ge(state_out, i)
                sbk = bank[1]
                mm(sbk[:, 0:128], mvtok[:, 0, hc], kw[:, 0, :], start=True, stop=False)
                mm(sbk[:, 0:128], mvtok[:, 1, hc], kw[:, 1, :], start=False, stop=True)
                mm(sbk[:, 128:256], mvtok[0:64, 2, hc], kw[0:64, 2, :], start=True, stop=True)
                mm(sbk[:, 256:257], kw[:, 0, :], ones[:, 0:1], start=True, stop=False)
                mm(sbk[:, 256:257], kw[:, 1, :], ones[:, 0:1], start=False, stop=True)
                mm(sbk[:, 257:258], kw[0:64, 2, :], ones[0:64, 0:1], start=True, stop=True).then_inc(state_ps, 1)

            def ml_norm(i):
                pe.wait_ge(hsq_ready, i + 1)
                if i:
                    pe.wait_ge(hrs_ready, i)
                mm(bank[7][:, 0:T], ones, scr[:, 5, 0:T], start=True, stop=True).then_inc(hss_ps, 1)

            for i in range(MLH):
                ml_scores(i)
                ada_tiles(2, lambda t: bank[0][:, 2 * t:2 * t + 2], ADA1 + 4 * i)
                if i:
                    ml_norm(i - 1)
                ml_values(i)
                ada_tiles(2, lambda t: bank[0][:, 2 * t:2 * t + 2], ADA1 + 4 * i + 2)
            ml_norm(MLH - 1)

            pe.wait_ge(mix_ready, 4)
            for t in range(8):
                if t % 2 == 0:
                    hold[0] = chunk()
                w = hold[0]
                if t >= 2:
                    pe.wait_ge(x1_ready, 2 * t - 2)
                for kk in range(KD):
                    last = mm(bank[4 + t % 2][:, 0:T], w[:, kk, (t % 2) * P:(t % 2 + 1) * P], mix[:, kk, :], start=kk == 0, stop=kk == KD - 1)
                last.then_inc(xo_ps, 1)
            for kk in range(KD):
                pe.wait_ge(x1sq_ready, kk + 1)
                last = mm(bank[7][:, 0:T], ones, h[:, kk, :], start=kk == 0, stop=kk == KD - 1)
            last.then_inc(ss2_ps, 1)
            assert used[0] == PRE

            pe.wait_ge(h2_ready, 16)
            for tt, (t0, n) in enumerate(TILES):
                for kk in range(KD):
                    last = mm(bank[6][0:n, tt * NE:(tt + 1) * NE], h[:, kk, t0:t0 + n], wrout[:, kk, :], start=kk == 0, stop=kk == KD - 1)
            last.then_inc(logit_ps, 1)
            for i in range(6):
                tt, half = i // 2, i % 2
                t0, n = TILES[tt]
                if i >= 2:
                    pe.wait_ge(r_ready, i - 1)
                for c in range(4):
                    last = nc.tensor.transpose(bank[i % 2][0:n, c * P:(c + 1) * P], h[:, half * 4 + c, t0:t0 + n], ident)
                last.then_inc(h2tr_ps, 1)
            pe.wait_ge(member_ready, 1)
            rb = bank[5]
            strict = mask_s[:, A]
            for tt in range(3):
                for u in range(tt + 1):
                    mm(rb[:, tt * NE:(tt + 1) * NE], strict if u == tt else ones, member[:, u, :], start=u == 0, stop=u == tt)
            for u in range(3):
                last = mm(rb[:, 96:128], ones, member[:, u, :], start=u == 0, stop=u == 2)
            last.then_inc(rank_ps, 1)
            pe.wait_ge(lo_ready, 6)

            X0, X1, U0, D0, R0 = 0, 1, 2, 4, 6

            def gather(turn):
                pe.wait_ge(pick_ready, turn * 3 + 3)
                if not isinstance(turn, int) or turn >= 1:
                    pe.wait_ge(xg_ready, turn * 2)
                if not isinstance(turn, int) or turn >= 2:
                    pe.wait_ge(spread_ready, turn - 1)
                for half in range(2):
                    gb = bank[X0 + half]
                    for c in range(4):
                        for tt, (t0, n) in enumerate(TILES):
                            for part in range(3):
                                last = mm(gb[:, c * CAP:(c + 1) * CAP], h2p[0:n, part, tt, (half * 4 + c) * P:(half * 4 + c + 1) * P],
                                          pick[0:n, tt, :], start=tt == 0 and part == 0, stop=tt == 2 and part == 2)
                    last.then_inc(gath_ps, 1)

            def weights(j, turn):
                slot, rounds = expert_turn(j)
                pe.wait_ge(slot_full[slot], (turn + (rounds + 1)) * 16)
                return ring[:, slot]

            def gate_up(j, turn, first):
                if j == 0:
                    pe.wait_ge(xg_ready, turn * 2 + 2)
                if not (first and j < 2):
                    pe.wait_ge(u_ready, turn * 4 + (j - 1))
                for part in range(2):
                    w = weights(2 * j + part, turn)
                    for i in range(2):
                        for kk in range(KD):
                            c0_ = (2 * part + i) * CAP
                            last = mm(bank[U0 + j % 2][:, c0_:c0_ + CAP], w[:, kk, i * P:(i + 1) * P], xg[:, kk, :],
                                      start=kk == 0, stop=kk == KD - 1)
                    last.then_inc(gu_ps if part else glu_used, 1)

            def down(turn, first):
                pe.wait_ge(act_ready, turn * 4 + 4)
                for m in range(4):
                    w = weights(8 + m, turn)
                    if m % 2 == 0 and not first:
                        pe.wait_ge(dn_ready, turn * 2 + (m // 2 - 1))
                    for i in range(2):
                        for kk in range(8):
                            c0_ = (2 * (m % 2) + i) * CAP
                            last = mm(bank[D0 + m // 2][:, c0_:c0_ + CAP], w[:, kk, i * P:(i + 1) * P], act[:, kk, :],
                                      start=kk == 0, stop=kk == 7)
                    last.then_inc(dn_ps if m % 2 else dn_used, 1)

            def back(turn):
                for half in range(2):
                    pe.wait_ge(dn_ready, turn * 2 + (half + 1))
                    pe.wait_ge(acc_ready, turn * 8 + 1)
                    for c in range(4):
                        last = nc.tensor.transpose(bank[R0 + half][0:CAP, c * P:(c + 1) * P], oT[:, half * 4 + c, :], ident)
                    last.then_inc(otr_ps, 1)
                pe.wait_ge(wpick_ready, turn * 3 + 3)
                for tt, (t0, n) in enumerate(TILES):
                    last = nc.tensor.transpose(bank[X0][0:CAP, t0:t0 + n], wpick[0:n, tt, :], ident[0:n, 0:n])
                last.then_inc(str_ps, 1)

            def scatter(half, turn):
                if half == 0:
                    pe.wait_ge(otok_ready, turn * 2 + 2)
                    pe.wait_ge(spread_ready, turn + 1)
                for c in range(half * 4, half * 4 + 4):
                    if c >= 2:
                        pe.wait_ge(acc_ready, turn * 8 + c)
                    mm(bank[R0 + c % 2][:, 0:T], otok[0:CAP, c * P:(c + 1) * P], spread[0:CAP, :], start=True, stop=True).then_inc(sc_ps, 1)

            def expert(turn, e, first, begins, ends):
                gate_up(0, turn, first)
                if not begins:
                    back(turn - 1)
                gate_up(1, turn, first)
                if not begins:
                    scatter(0, turn - 1)
                gate_up(2, turn, first)
                if not begins:
                    scatter(1, turn - 1)
                gate_up(3, turn, first)
                if not ends:
                    gather(turn + 1)
                down(turn, first)

            def finish(turn):
                back(turn)
                scatter(0, turn)
                scatter(1, turn)

            passes(pe, lambda turn, e, b: gather(turn), expert, finish)

        @block.scalar
        def _(act_):
            chain = Chain(act_, a_chain)
            fn = nc.scalar.activation
            a_one = ones[:, 0:1]

            def copy(out, in_):
                return fn(out, in_, ACT.Copy)

            for dst, src in ((ssb[:], small), (csb[:], const), (x[:], xT.rearrange("(k p) t -> p k t", p=P)),
                             (wgate[:], w_in.rearrange("o (k p) n -> (o p) k n", p=P)[:, :, 3072:3080])):
                act_.dma_start(dst, src).then_inc(ld_small, 16)
            for dst, src in ((kc, kcT.rearrange("(c p) n -> p c n", p=P)), (vpast, vc)):
                act_.dma_start(dst, src).then_inc(ld_side, 16)
            act_.wait_ge(ld_small, 16 * 4)
            c_in = Sm("cT").rearrange("p (k s) -> p k s", k=KD)
            fn(cs, c_in, ACT.Sigmoid).then_inc(csig, 1)
            fn(sq, x[:], ACT.Square).then_inc(xsq_ready, 1)

            def rstd(out, ps, n, ready):
                chain(fn(out, ps, ACT.Ln, bias=eps, scale=1.0 / n))
                fn(out, out, ACT.Exp, scale=-0.5).then_inc(ready, 1)

            act_.wait_ge(ss1_ps, 1)
            rstd(scr[:, 2, 0:T], bank[7][:, 0:T], D, rstd1_ready)
            act_.wait_ge(mod1_ready, 1)
            for kk in range(KD):
                act_.wait_ge(hs_ready, 2 * kk + 2)
                for cols, sq_ in SEQ:
                    fn(h[:, kk, cols], h[:, kk, cols], ACT.Identity, bias=mod[:, kk, sq_:sq_ + 1]).then_inc(h_ready, 1)

            dst = [q[:, c, :] for c in range(4)] + [k[:, c, 0:T] for c in range(4)] + [vT[:, c, :] for c in range(4)]
            dst += [raw[:, c, :] for c in range(8)] + [mvT[:, c, :] for c in range(4)] + [mo_g[:, c, :] for c in range(4)]

            def proj_out(t):
                act_.wait_ge(proj_ps, t + 1)
                pb = bank[t % 2]
                if t < 8:
                    copy(dst[t], pb[:, 0:T])
                    if t >= 2:
                        act_.wait_ge(nss_ps, t - 1)
                    fn(scr[:, t % 2, 0:T], pb[:, 0:T], ACT.Square).then_inc(sq_ready, 1)
                elif 12 <= t < 20:
                    copy(dst[t][:, CW - 1:CW - 1 + TP], pb[:, 0:TP])
                    copy(dst[t][:, CS + CW - 1:RAWW], pb[:, TP:T]).then_inc(proj_done, 1)
                else:
                    copy(dst[t], pb[:, 0:T]).then_inc(proj_done, 1)

            def nrs(i):
                act_.wait_ge(nss_ps, i + 1)
                if i >= 2:
                    act_.wait_ge(qk_ready, i - 1)
                rstd(scr[:, 2 + i % 2, 0:T], bank[6 + i % 2][:, 0:T], SBD, nrs_ready)

            act_.wait_ge(v_init, 3)
            for t in range(12):
                proj_out(t)
                if 1 <= t < 9:
                    nrs(t - 1)
            act_.wait_ge(proj_done, 4)
            act_.dma_start(voT.rearrange("(c p) t -> p c t", p=P), vT).then_inc(sb_stored, 16)
            act_.wait_ge(qk_ready, 8)
            act_.dma_start(koT.rearrange("(c p) t -> p c t", p=P), k[:, :, 0:T]).then_inc(sb_stored, 16)

            act_.wait_ge(frow_ready, 1)
            chain(fn(rows[0:MLH, 2, :], rows[0:MLH, 1, :], ACT.Abs))
            chain(fn(rows[0:MLH, 2, :], rows[0:MLH, 2, :], ACT.Exp, scale=-1.0))
            fn(rows[0:MLH, 2, :], rows[0:MLH, 2, :], ACT.Ln, bias=a_one[0:MLH]).then_inc(flog_ready, 1)

            for i in range(SBH + 1):
                if i >= 1:
                    act_.wait_ge(t_ready, i)
                    tt_ = scr[:, 3 * ((i - 1) % 2) + 2, :]
                    fn(tt_, tt_, ACT.Exp).then_inc(e_ready, 1)
                if i < SBH:
                    act_.wait_ge(z_ps, i + 1)
                    l = scr[:, 3 * (i % 2), :]
                    chain(fn(l, bank[2 + i % 2][:, :], ACT.Abs))
                    chain(fn(l, l, ACT.Exp, scale=-1.0))
                    fn(l, l, ACT.Ln, bias=a_one).then_inc(l_ready, 1)
                    proj_out(12 + 2 * i)
                    proj_out(13 + 2 * i)

            act_.wait_ge(proj_done, 20)
            cv = convo.rearrange("(c p) s w -> p c s w", p=P)
            with nc.allow_non_contiguous_dma(reason="three columns of each row"):
                act_.dma_start(cv[:, :, 0, :], raw[:, :, TP:TP + 3]).then_inc(conv_stored, 16)
                act_.dma_start(cv[:, :, 1, :], raw[:, :, RAWW - 3:RAWW]).then_inc(conv_stored, 16)
            act_.wait_ge(conv_ready, 8)
            act_.wait_ge(conv_stored, 32)
            fn(sgy, y, ACT.Sigmoid)
            fn(mo_g, mo_g, ACT.Sigmoid).then_inc(sgy_ready, 1)
            act_.wait_ge(mkq_ready, 1)
            act_.dma_start(C0, c0).then_inc(ld_state, 16)
            act_.dma_start(C0T, c0T).then_inc(ld_state, 16)
            act_.wait_ge(rows_ready, 1)
            with nc.allow_non_contiguous_dma(reason="one element per head"):
                act_.dma_start(mo, rows[0:MLH, 3, TP - 1:T:TS]).then_inc(state_stored, 16)
            for tt, (t0, n) in enumerate(TILES):
                act_.wait_ge(mvtr_ps, tt + 1)
                copy(mvtok[0:n, tt, :], bank[3 + tt][0:n, :]).then_inc(mvtok_ready, 1)

            def hrs(i):
                act_.wait_ge(hss_ps, i + 1)
                rstd(scr[:, 5, 0:T], bank[7][:, 0:T], MLD, hrs_ready)

            for i in range(MLH):
                act_.wait_ge(mt_ps, i + 1)
                fn(scr[:, 4, 0:T], bank[4][:, 0:T], ACT.Exp, scale=-1.0)
                act_.wait_ge(wtmp_ready, i + 1)
                fn(scr[:, 0, ACBE], scr[:, 0, ACBE], ACT.Exp, scale=-1.0)
                fn(scr[:, 3, 192:256], bank[3][:, TP:T], ACT.Exp, bias=Sm("m0b")[:, i:i + 1], scale=-1.0).then_inc(w_ready, 1)
                if i:
                    hrs(i - 1)
                act_.wait_ge(hd_ready, i + 1)
                fn(scr[:, 5, 0:T], hh, ACT.Square).then_inc(hsq_ready, 1)
            hrs(MLH - 1)
            act_.wait_ge(state_out, MLH)
            act_.dma_start(co.rearrange("s h v k -> v (s h) k"), Cout.rearrange("p s h k -> p (s h) k")).then_inc(state_stored, 16)
            act_.dma_start(no, nout.rearrange("p s h -> p (s h)")).then_inc(state_stored, 16)

            for kk in range(KD):
                act_.wait_ge(x1_ready, 2 * kk + 2)
                fn(h[:, kk, :], x[:, kk, :], ACT.Square).then_inc(x1sq_ready, 1)
            act_.dma_start(bgu, b_gu).then_inc(ld_bias, 16)
            act_.dma_start(bdn, b_down).then_inc(ld_bias, 16)
            act_.wait_ge(ss2_ps, 1)
            rstd(scr[:, 2, 0:T], bank[7][:, 0:T], D, rstd2_ready)
            act_.wait_ge(mod2_ready, 1)
            for kk in range(KD):
                act_.wait_ge(hs2_ready, 2 * kk + 2)
                for cols, sq_ in SEQ:
                    fn(h[:, kk, cols], h[:, kk, cols], ACT.Identity, bias=mod[:, 24 + kk, sq_:sq_ + 1]).then_inc(h2_ready, 1)
            act_.wait_ge(top_ready, 1)
            for tt in range(3):
                fn(gate[:, tt, :], lg[:, tt, :], ACT.Exp, bias=negv[:, tt:tt + 1]).then_inc(ex_ready, 1)
            for i in range(6):
                tt, half = i // 2, i % 2
                n = TILES[tt][1]
                hc = slice(half * 512, half * 512 + 512)
                act_.wait_ge(h2tr_ps, i + 1)
                copy(h2p[0:n, 0, tt, hc], bank[i % 2][0:n, :]).then_inc(hi_ready, 1)
                act_.wait_ge(r_ready, i + 1)
                copy(h2p[0:n, 1, tt, hc], res[0:n, i % 2, :]).then_inc(mid_ready, 1)

            def gathered(turn):
                for half in range(2):
                    act_.wait_ge(gath_ps, turn * 2 + (half + 1))
                    copy(xg[:, half * 4:half * 4 + 4, :], bank[half][:, 0:4 * CAP].rearrange("p (c n) -> p c n", c=4)).then_inc(xg_ready, 1)

            def sigm(j, turn):
                act_.wait_ge(gc_ready, turn * 4 + (j + 1))
                fn(sg, gc, ACT.Sigmoid, scale=SWIGLU_ALPHA).then_inc(sg_ready, 1)

            def turned(turn):
                for half in range(2):
                    act_.wait_ge(otr_ps, turn * 2 + (half + 1))
                    copy(otok[0:CAP, half * 512:half * 512 + 512], bank[6 + half][0:CAP, :]).then_inc(otok_ready, 1)
                act_.wait_ge(str_ps, turn + 1)
                copy(spread[0:CAP, :], bank[0][0:CAP, 0:T]).then_inc(spread_ready, 1)

            def expert(turn, e, first, begins, ends):
                sigm(0, turn)
                if not begins:
                    turned(turn - 1)
                sigm(1, turn)
                sigm(2, turn)
                sigm(3, turn)
                if not ends:
                    gathered(turn + 1)

            passes(act_, lambda turn, e, b: gathered(turn), expert, turned)

        @block.vector
        def _(v):
            chain = Chain(v, v_chain)
            ts, tt_, stt, cp = nc.vector.tensor_scalar, nc.vector.tensor_tensor, nc.vector.scalar_tensor_tensor, nc.vector.tensor_copy
            v.wait_ge(ld_small, 16 * 4)
            nc.vector.memset(k[:, :, T:384], 0.0).then_inc(v_init, 1)
            nc.vector.memset(raw[:, :, 0:CW - 1], 0.0).then_inc(v_init, 1)
            cp(raw[:, :, CW - 1 + TP:CS + CW - 1], Sm("conv_past").rearrange("p (c w) -> p c w", c=8)).then_inc(v_init, 1)
            chain.step(ts(gqs, Sm("gq"), SBD ** -0.5, None, ALU.mult))
            nc.vector.memset(acol[64:128, 2, :], 0.0)
            v.wait_ge(csig, 1)
            tt_(cs, Sm("cT").rearrange("p (k s) -> p k s", k=KD), cs, ALU.mult).then_inc(cs_ready, 1)

            def mod_of(t0, t1, ps):
                return tt_(mod[:, t0:t1, :], ps[:, 2 * t0:2 * t1].rearrange("p (t s) -> p t s", s=2),
                           Sm("b_ada")[:, t0:t1].unsqueeze(2).broadcast_to([P, t1 - t0, 2]), ALU.add)

            def scaled(out, t0, g):
                return stt(out, mod[:, t0:t0 + KD, :], 1.0, Sm(g).unsqueeze(2).broadcast_to([P, KD, 2]), ALU.add, ALU.mult)

            v.wait_ge(ada_used, ADA1)
            mod_of(0, 16, bank[2]).then_inc(mod1_ready, 1)
            v.wait_ge(mod1_ready, 1)
            chain(scaled(s1, 8, "g1"))
            v.wait_ge(rstd1_ready, 1)
            for kk in range(KD):
                for cols, sq_ in SEQ:
                    stt(h[:, kk, cols], x[:, kk, cols], s1[:, kk, sq_:sq_ + 1], scr[:, 2, cols], ALU.mult, ALU.mult).then_inc(hs_ready, 1)

            for i in range(8):
                dst = q[:, i, :] if i < 4 else k[:, i - 4, 0:T]
                v.wait_ge(nrs_ready, i + 1)
                stt(dst, dst, gqs if i < 4 else Sm("gk"), scr[:, 2 + i % 2, 0:T], ALU.mult, ALU.mult).then_inc(qk_ready, 1)
            v.wait_ge(gates_ps, 1)
            cp(gtok[:, 0:2, :], bank[5][:, 0:16].rearrange("p (t g) -> p t g", t=2))
            cp(gtok[0:64, 2, :], bank[5][0:64, 16:24]).then_inc(gtok_ready, 1)
            for tt, (t0, n) in enumerate(TILES):
                v.wait_ge(vtr_ps, tt + 1)
                cp(vtok[0:n, tt, :], bank[2 + tt][0:n, :]).then_inc(vtok_ready, 1)
            v.wait_ge(grow_ps, 1)
            r4 = slice(0, MLH)
            chain.step(ts(rows[r4, 0, :], bank[6][r4, 0:T], Sm("bgate")[r4, 0:1], None, ALU.add))
            ts(rows[r4, 1, :], bank[7][r4, 0:T], Sm("bgate")[r4, 1:2], None, ALU.add).then_inc(frow_ready, 1)

            def gate_rows():
                v.wait_ge(flog_ready, 1)
                chain(stt(rows[r4, 1, :], rows[r4, 1, :], 0.0, rows[r4, 2, :], ALU.min, ALU.subtract))
                one = ones[r4, 0:1]
                for cols, sq_ in SEQ:
                    n = cols.stop - cols.start
                    chain.step(nc.vector.tensor_tensor_scan(rows[r4, 2, cols], one.broadcast_to([MLH, n]), rows[r4, 1, cols], 0.0, ALU.mult, ALU.add))
                chain.wait()
                chain(tt_(rows[r4, 0, :], rows[r4, 0, :], rows[r4, 2, :], ALU.subtract))
                for cols, sq_ in SEQ:
                    n = cols.stop - cols.start
                    chain.step(nc.vector.tensor_tensor_scan(rows[r4, 1, cols], one.broadcast_to([MLH, n]), rows[r4, 0, cols],
                                                            Sm("m0c")[r4, :] if sq_ else 0.0, ALU.mult, ALU.max))
                chain.wait()
                tt_(rows[r4, 3, :], rows[r4, 2, :], rows[r4, 1, :], ALU.add).then_inc(rows_ready, 1)

            def conv(j):
                wc = Sm("w_conv")[:, j * CW:(j + 1) * CW]
                v.wait_ge(proj_done, 5 + j)
                chain(ts(y[:, j, :], raw[:, j, 0:CONVW], wc[:, 0:1], Sm("b_conv")[:, j:j + 1], ALU.mult, ALU.add))
                for tap in range(1, CW):
                    ins = stt(y[:, j, :], raw[:, j, tap:tap + CONVW], wc[:, tap:tap + 1], y[:, j, :], ALU.mult, ALU.add)
                    if tap < CW - 1:
                        chain(ins)
                    else:
                        ins.then_inc(conv_ready, 1)

            for i in range(SBH + 2):
                if 1 <= i <= SBH:
                    v.wait_ge(between_ps, i)
                    t_ = scr[:, 3 * ((i - 1) % 2) + 2, :]
                    chain.wait()
                    tt_(t_, t_, bank[4 + (i - 1) % 2][:, :], ALU.subtract).then_inc(t_ready, 1)
                if i >= 3 and i % 2:
                    v.wait_ge(av_ps, i - 1)
                    cp(mix[:, (i - 3) // 2, :], bank[6][:, 0:T]).then_inc(av_done, 1)
                if i < SBH:
                    v.wait_ge(l_ready, i + 1)
                    b3 = 3 * (i % 2)
                    zb = bank[2 + i % 2][:, :]
                    stt(scr[:, b3 + 1, :], zb, 0.0, scr[:, b3, :], ALU.max, ALU.add).then_inc(sp_ready, 1)
                    if i >= 2:
                        v.wait_ge(av_ps, i - 1)
                    chain.step(stt(scr[:, b3 + 2, :], zb, 0.0, scr[:, b3, :], ALU.min, ALU.subtract))
                if 1 <= i <= 4:
                    conv(2 * i - 2)
                    conv(2 * i - 1)
                if i == 5:
                    gate_rows()

            v.wait_ge(sb_stored, 32)
            v.wait_ge(sgy_ready, 1)
            for cols, src in ((slice(0, TP), slice(0, TP)), (slice(TP, T), slice(CS, CONVW))):
                tt_(mq[:, :, cols], y[:, 0:4, src], sgy[:, 0:4, src], ALU.mult)
                stt(mk[:, :, cols], y[:, 4:8, src], MLD ** -0.5, sgy[:, 4:8, src], ALU.mult, ALU.mult)
            nc.vector.memset(mk[:, :, T:384], 0.0).then_inc(mkq_ready, 1)
            for tt, (t0, n) in enumerate(TILES):
                v.wait_ge(ktr_ps, tt + 1)
                cp(mktok[0:n, tt, :], bank[tt][0:n, :]).then_inc(ktok_ready, 1)
            v.wait_ge(acol_ps, 1)
            cp(acol[:, 0:2, :], bank[6][:, 0:8].rearrange("p (t h) -> p t h", t=2))
            cp(acol[0:64, 2, :], bank[6][0:64, 8:12]).then_inc(acol_ready, 1)
            v.wait_ge(acol_ready, 1)
            v.wait_ge(ld_state, 32)

            def ml_weights(i):
                Mb = bank[3]
                v.wait_ge(mb_ps, i + 1)
                ts(scr[:, 0, AC], Mb[:, 0:256], acol[:, 0, i:i + 1], 0.0, ALU.subtract, ALU.max)
                ts(scr[:, 0, B], Mb[:, 128:256], acol[:, 1, i:i + 1], 0.0, ALU.subtract, ALU.max)
                ts(scr[:, 0, E], Mb[:, 256:320], acol[:, 2, i:i + 1], 0.0, ALU.subtract, ALU.max).then_inc(wtmp_ready, 1)
                v.wait_ge(w_ready, i + 1)
                v.wait_ge(st_ps, i + 1)
                tt_(scr[:, 1, ACBE], bank[2][:, ACBE], scr[:, 0, ACBE], ALU.mult).then_inc(s_ready, 1)
                tt_(scr[:, 3, 0:64], mq[:, i, TP:T], scr[:, 3, 192:256], ALU.mult)
                ts(scr[:, 3, 64:192], ones, Sm("n0")[:, i:i + 1], None, ALU.mult).then_inc(qw_ready, 1)
                hc = slice(i * P, (i + 1) * P)
                ts(scr[:, 2, 0:128], mktok[:, 0, hc], scr[:, 0, 255:256], None, ALU.mult)
                ts(scr[:, 2, 128:256], mktok[:, 1, hc], scr[:, 0, 383:384], None, ALU.mult)
                ts(scr[0:64, 2, 256:384], mktok[0:64, 2, hc], scr[0:64, 0, 447:448], None, ALU.mult).then_inc(kw_ready, 1)

            def ml_out(i):
                v.wait_ge(hrs_ready, i + 1)
                chain(tt_(hh, hh, scr[:, 5, 0:T], ALU.mult))
                stt(mix[:, 4 + i, :], hh, Sm("gh"), mo_g[:, i, :], ALU.mult, ALU.mult).then_inc(mix_ready, 1)

            def ml_hidden(i):
                v.wait_ge(num_ps, i + 1)
                den = scr[:, 4, 0:T]
                chain(tt_(den, bank[6][:, 0:T], den, ALU.max))
                chain(stt(den, bank[6][:, 0:T], -1.0, den, ALU.mult, ALU.max))
                chain(nc.vector.reciprocal(den, den))
                tt_(hh, bank[5][:, 0:T], den, ALU.mult).then_inc(hd_ready, 1)
                v.wait_ge(hd_ready, i + 1)
                v.wait_ge(state_ps, i + 1)
                dec = scr[:, 3, 255:256]
                cp(Cout[:, 0, i, :], bank[1][:, 0:128])
                stt(Cout[:, 1, i, :], C0[:, i, :], dec, bank[1][:, 128:256], ALU.mult, ALU.add)
                cp(nout[:, 0, i:i + 1], bank[1][:, 256:257])
                stt(nout[:, 1, i:i + 1], Sm("n0")[:, i:i + 1], dec, bank[1][:, 257:258], ALU.mult, ALU.add).then_inc(state_out, 1)

            for i in range(MLH + 1):
                if i < MLH:
                    ml_weights(i)
                if i:
                    ml_out(i - 1)
                if i < MLH:
                    ml_hidden(i)

            v.wait_ge(ada_used, ADA1 + ADA2)
            mod_of(16, 48, bank[0]).then_inc(mod2_ready, 1)
            v.wait_ge(mod2_ready, 1)
            chain(scaled(s2, 32, "g2"))
            for t in range(8):
                v.wait_ge(xo_ps, t + 1)
                for cols, sq_ in SEQ:
                    stt(x[:, t, cols], bank[4 + t % 2][:, cols], mod[:, 16 + t, sq_:sq_ + 1], x[:, t, cols], ALU.mult, ALU.add).then_inc(x1_ready, 1)
            v.wait_ge(rstd2_ready, 1)
            v.wait_ge(x1_ready, 16)
            for kk in range(KD):
                for cols, sq_ in SEQ:
                    stt(h[:, kk, cols], x[:, kk, cols], s2[:, kk, sq_:sq_ + 1], scr[:, 2, cols], ALU.mult, ALU.mult).then_inc(hs2_ready, 1)

            nc.vector.memset(lg[64:128, 2, :], 0.0)
            v.wait_ge(logit_ps, 1)
            br = Sm("b_router")
            tt_(lg[:, 0:2, :], bank[6][:, 0:64].rearrange("p (t e) -> p t e", t=2), br.unsqueeze(1).broadcast_to([P, 2, NE]), ALU.add)
            chain(tt_(lg[0:64, 2, :], bank[6][0:64, 64:96], br[0:64, :], ALU.add))
            for tt in range(3):
                chain.step(nc.vector.max(top[:, tt, :], lg[:, tt, :]))
            chain.wait()
            for tt in range(3):
                chain.step(nc.vector.max_index(topi[:, tt, :], top[:, tt, :], lg[:, tt, :]))
            chain.wait()
            cp(topf, topi)
            ts(negv, top[:, :, 0], -1.0, None, ALU.mult).then_inc(top_ready, 1)
            v.wait_ge(top_ready, 1)
            for i in range(TOPK):
                for tt in range(3):
                    if i == 0:
                        chain.step(ts(member[:, tt, :], iota_e, topf[:, tt, 0:1], None, ALU.is_equal))
                    else:
                        chain.step(stt(member[:, tt, :], iota_e, topf[:, tt, i:i + 1], member[:, tt, :], ALU.is_equal, ALU.add))
                chain.wait()
            nc.vector.memset(member[64:128, 2, :], 0.0).then_inc(member_ready, 1)
            for i in range(6):
                tt, half = i // 2, i % 2
                n = TILES[tt][1]
                hc = slice(half * 512, half * 512 + 512)
                v.wait_ge(hi_ready, i + 1)
                tt_(res[0:n, i % 2, :], bank[i % 2][0:n, :], h2p[0:n, 0, tt, hc], ALU.subtract).then_inc(r_ready, 1)
                v.wait_ge(mid_ready, i + 1)
                tt_(h2p[0:n, 2, tt, hc], res[0:n, i % 2, :], h2p[0:n, 1, tt, hc], ALU.subtract).then_inc(lo_ready, 1)
            v.wait_ge(member_ready, 1)
            v.wait_ge(ex_ready, 3)
            chain(tt_(gate[:], gate[:], member[:], ALU.mult))
            chain(nc.vector.reduce_sum(rs4, gate[:], AX_X))
            chain(ts(rs4, rs4, 0.5, None, ALU.max))
            chain(nc.vector.reciprocal(rs4, rs4))
            chain(tt_(gate[:], gate[:], rs4.unsqueeze(2).broadcast_to([P, 3, NE]), ALU.mult))
            v.wait_ge(rank_ps, 1)
            chain(stt(rank[:], bank[5][:, 0:96].rearrange("p (t e) -> p t e", t=3), 1.0, member[:], ALU.add, ALU.mult))
            chain(ts(rank[:], rank[:], -1.0, None, ALU.add))
            chain(nc.vector.reduce_max(cmax, bank[5][:, 96:128], AX_X))
            cp(cmaxi, cmax).then_inc(cnt_ready, 1)
            v.wait_ge(state_stored, 16 * 3)
            v.wait_ge(x1_ready, 16)
            nc.vector.memset(acc, 0.0).then_inc(acc_ready, 1)

            def picks(turn, e):
                for tt, (t0, n) in enumerate(TILES):
                    ts(pick[0:n, tt, :], iota_c[0:n], rank[0:n, tt, bass.ds(e, 1)], None, ALU.is_equal).then_inc(pick_ready, 1)

            def wpicks(turn, e):
                for tt, (t0, n) in enumerate(TILES):
                    ts(wpick[0:n, tt, :], iota_c[0:n], rank[0:n, tt, bass.ds(e, 1)], gate[0:n, tt, bass.ds(e, 1)],
                           ALU.is_equal, ALU.mult).then_inc(wpick_ready, 1)

            def glu(j, turn, e):
                v.wait_ge(gu_ps, turn * 4 + (j + 1))
                bias = bgu[:, bass.ds(e, 1), 4 * j:4 * j + 4].rearrange("p a b -> p (a b)").unsqueeze(2).broadcast_to([P, 4, CAP])
                tt_(ub, bank[2 + j % 2][:, 0:4 * CAP].rearrange("p (c n) -> p c n", c=4), bias, ALU.add).then_inc(u_ready, 1)
                v.wait_ge(u_ready, turn * 4 + (j + 1))
                ts(gc, ub[:, 0:2, :], SWIGLU_LIMIT, None, ALU.min).then_inc(gc_ready, 1)
                ts(lc, ub[:, 2:4, :], SWIGLU_LIMIT, -SWIGLU_LIMIT, ALU.min, ALU.max).then_inc(lc_ready, 1)
                v.wait_ge(lc_ready, turn * 4 + (j + 1))
                stt(lc, lc, 1.0, gc, ALU.add, ALU.mult).then_inc(gl_ready, 1)
                v.wait_ge(gl_ready, turn * 4 + (j + 1))
                v.wait_ge(sg_ready, turn * 4 + (j + 1))
                tt_(act[:, 2 * j:2 * j + 2, :], lc, sg, ALU.mult).then_inc(act_ready, 1)

            def add(half, turn):
                v.wait_ge(acc_ready, turn * 8 + 1)
                for c in range(half * 4, half * 4 + 4):
                    v.wait_ge(sc_ps, turn * 8 + (c + 1))
                    tt_(acc[:, c, :], bank[6 + c % 2][:, 0:T], acc[:, c, :], ALU.add).then_inc(acc_ready, 1)

            def start(turn, e, b):
                if not isinstance(b, int):
                    ts(rank[:], rank[:], float(-CAP), None, ALU.add).then_inc(rank_moved, 1)
                    v.wait_ge(rank_moved, b)
                picks(turn, e)

            def expert(turn, e, first, begins, ends):
                glu(0, turn, e)
                if not ends:
                    picks(turn + 1, e + 1)
                glu(1, turn, e)
                wpicks(turn, e)
                if not begins:
                    add(0, turn - 1)
                glu(2, turn, e)
                if not begins:
                    add(1, turn - 1)
                glu(3, turn, e)
                for half in range(2):
                    v.wait_ge(dn_ps, turn * 2 + (half + 1))
                    bias = bdn[:, bass.ds(e, 1), 4 * half:4 * half + 4].rearrange("p a b -> p (a b)").unsqueeze(2).broadcast_to([P, 4, CAP])
                    tt_(oT[:, 4 * half:4 * half + 4, :], bank[4 + half][:, 0:4 * CAP].rearrange("p (c n) -> p c n", c=4), bias, ALU.add).then_inc(dn_ready, 1)

            def finish(turn):
                add(0, turn)
                add(1, turn)

            v.wait_ge(ld_bias, 32)
            passes(v, start, expert, finish)
            nc.vector.memset(cmax, 0.0).then_inc(acc_closed, 1)
            v.wait_ge(acc_closed, 1)
            for kk in range(KD):
                for cols, sq_ in SEQ:
                    stt(h[:, kk, cols], acc[:, kk, cols], mod[:, 40 + kk, sq_:sq_ + 1], x[:, kk, cols], ALU.mult, ALU.add).then_inc(y_ready, 1)

        @block.gpsimd
        def _(g):
            g.wait_ge(ld_small, 64)

            def masked(buf, mask, ready):
                nc.gpsimd.tensor_tensor(scr[:, buf, A], scr[:, buf, A], mask[:, A], ALU.mult)
                nc.gpsimd.tensor_tensor(scr[:, buf, BE], scr[:, buf, BE], mask[:, BE], ALU.mult).then_inc(ready, 1)

            for i in range(SBH + 1):
                if i:
                    g.wait_ge(e_ready, i)
                    masked(3 * ((i - 1) % 2) + 2, mask_s, a_ready)
                if i < SBH:
                    g.wait_ge(sp_ready, i + 1)
                    masked(3 * (i % 2) + 1, mask_s, spm_ready)
            for i in range(MLH):
                g.wait_ge(s_ready, i + 1)
                masked(1, mask_i, sm_ready)


_OUTS = (("yT", (D, T)), ("koT", (512, T)), ("voT", (512, T)), ("convo", (D, 2, 3)), ("co", (2, MLH, P, P)),
         ("no", (P, 2 * MLH)), ("mo", (MLH, 2)))


def constants():
    c = np.zeros((P, NCONST), np.float32)

    def put(name, a):
        c[:a.shape[0], CONST[name][0]:CONST[name][0] + a.shape[1]] = a
    i = np.arange(P)
    put("ident", np.eye(P, dtype=np.float32))
    put("ones", np.ones((P, P), np.float32))
    put("tri", (i[:, None] > i[None, :]).astype(np.float32))
    put("blk", (i[:, None] // SBD == i[None, :] // SBD).astype(np.float32))
    for name, before in (("mask_s", i[:, None] < i[None, :]), ("mask_i", i[:, None] <= i[None, :])):
        m = np.zeros((P, 448), np.float32)
        m[:, A] = before
        m[:, C] = 1
        m[:, B] = before
        m[:64, E] = before[:64, :64]
        put(name, m)
    sel = np.zeros((MLH, MLH, P), np.float32)
    for j in range(MLH):
        sel[j, j] = 1
    put("sel", sel.reshape(MLH, MLH * P))
    put("iota_e", np.tile(np.arange(NE, dtype=np.float32), (P, 1)))
    put("iota_c", np.tile(np.arange(CAP, dtype=np.float32), (P, 1)))
    return c


def kernel(x_prompt, x_sample, c_prompt, c_sample, cache_sb_k, cache_sb_v, state_conv, state_mlstm_c,
           state_mlstm_n, state_mlstm_m, w_ada, b_ada, g_norm1, w_in, g_q, g_k, w_conv, b_conv, b_gate,
           g_head, w_out, g_norm2, w_router, b_router, w_gu, b_gu, w_down, b_down):
    import concourse.bacc as bacc
    from concourse.bass_utils import run_bass_kernel_spmd

    def A_(a):
        return np.asarray(a)

    small = np.zeros((P, NSMALL), np.float32)

    def put(name, a):
        a = np.asarray(a)
        small[:a.shape[0], SMALL[name][0]:SMALL[name][0] + a.shape[1]] = a

    put("g1", A_(g_norm1)[0].reshape(KD, P).T)
    put("g2", A_(g_norm2)[0].reshape(KD, P).T)
    put("b_ada", A_(b_ada)[0].reshape(48, P).T)
    put("b_conv", A_(b_conv)[0].reshape(8, P).T)
    put("w_conv", A_(w_conv)[0].reshape(CW, 8, P).transpose(2, 1, 0).reshape(P, 8 * CW))
    put("gq", np.tile(A_(g_q)[0], 2)[:, None])
    put("gk", np.tile(A_(g_k)[0], 2)[:, None])
    put("gh", A_(g_head)[0][:, None])
    put("n0", A_(state_mlstm_n)[0, 0].T)
    put("cT", np.stack([A_(c_prompt)[0].reshape(KD, P), A_(c_sample)[0].reshape(KD, P)], -1).transpose(1, 0, 2).reshape(P, 16))
    put("m0b", np.tile(A_(state_mlstm_m)[0, 0][None, :], (P, 1)))
    put("m0c", A_(state_mlstm_m)[0, 0][:, None])
    put("b_router", np.tile(A_(b_router)[0][None, :], (P, 1)))
    put("eps", np.full((P, 1), 1e-6, np.float32))
    put("conv_past", A_(state_conv)[0, 0].reshape(3, 8, P).transpose(2, 1, 0).reshape(P, 24))
    put("bgate", A_(b_gate)[0].reshape(2, MLH).T)
    put("w_router", A_(w_router)[0].reshape(KD, P, NE).transpose(1, 0, 2).reshape(P, KD * NE))
    c0_ = A_(state_mlstm_c)[0, 0]
    arrays = {
        "xT": np.concatenate([A_(x_prompt)[0], A_(x_sample)[0]], 0).T,
        "small": small,
        "const": constants(),
        "b_gu": A_(b_gu)[0].reshape(NE, 2, 4, 2, P).transpose(4, 0, 2, 1, 3).reshape(P, NE, 16),
        "b_down": A_(b_down)[0].reshape(NE, 8, P).transpose(2, 0, 1),
        "kcT": A_(cache_sb_k)[0, 0].reshape(PAST, 512).T,
        "vc": A_(cache_sb_v)[0, 0].reshape(PAST, 512),
        "c0": c0_.transpose(1, 0, 2),
        "c0T": c0_.transpose(2, 0, 1),
        "w_ada": A_(w_ada), "w_in": A_(w_in), "w_out": A_(w_out), "w_gu": A_(w_gu), "w_down": A_(w_down),
    }
    arrays = {n: np.ascontiguousarray(a) for n, a in arrays.items()}
    nc = bacc.Bacc("TRN2", target_bir_lowering=False, num_devices=1)
    args = [nc.dram_tensor(n, a.shape, mybir.dt.from_np(a.dtype), kind="ExternalInput").ap() for n, a in arrays.items()]
    args += [nc.dram_tensor(n, shape, F32, kind="ExternalOutput").ap() for n, shape in _OUTS]
    build(nc, *args)
    r = run_bass_kernel_spmd(nc, [arrays], core_ids=[0]).results[0]
    y = np.ascontiguousarray(r["yT"].T)
    kk = np.ascontiguousarray(r["koT"].T).reshape(T, SBH, SBD)
    vv = np.ascontiguousarray(r["voT"].T).reshape(T, SBH, SBD)
    cv = r["convo"].transpose(1, 2, 0)
    n = r["no"].reshape(P, 2, MLH).transpose(1, 2, 0)
    m = r["mo"].T

    def out(a):
        return np.ascontiguousarray(a)[None, None]
    return (y[None, :TP], y[None, TP:], out(kk[:TP]), out(vv[:TP]), out(cv[0]), out(r["co"][0]), out(n[0]), out(m[0]),
            out(kk[TP:]), out(vv[TP:]), out(cv[1]), out(r["co"][1]), out(n[1]), out(m[1]))
```

```python
from contextlib import ExitStack

import numpy as np
import concourse.bass as bass
from concourse import mybir

ALU = mybir.AluOpType
ACT = mybir.ActivationFunctionType
AX_X = mybir.AxisListType.X
F32 = mybir.dt.float32
BF16 = mybir.dt.bfloat16
U32 = mybir.dt.uint32
I32 = mybir.dt.int32

P = 128
D = 1024
KD = D // P
TP, TS = 256, 64
T = TP + TS
TILES = ((0, 128), (128, 128), (256, 64))
PAST = 128
SBH, SBD = 8, 64
MLH, MLD = 4, 128
CW = 4
RAWW = CW - 1 + TP + CW - 1 + TS
CONVW = RAWW - (CW - 1)
CS = TP + CW - 1
NE, TOPK = 32, 4
CAP = 128
SWIGLU_LIMIT, SWIGLU_ALPHA = 7.0, 1.702

CHC = 512
SLOTS = 6
ADA1, SBP, MLP, ADA2, WO = 4, 3, 4, 8, 2
PRE = ADA1 + SBP + MLP + ADA2 + WO
SHIFT = -PRE % SLOTS
PASSES = -(-T // CAP)

A, C, B, E, DP = slice(0, 128), slice(128, 256), slice(256, 384), slice(384, 448), slice(448, 512)
AC, BE, ACBE = slice(0, 256), slice(256, 448), slice(0, 448)

SMALL = {}
_at = 0
for _n, _w in (("g1", 8), ("g2", 8), ("b_ada", 48), ("b_conv", 8), ("w_conv", 8 * CW), ("gq", 1), ("gk", 1), ("gh", 1),
               ("n0", MLH), ("cT", 16), ("m0b", MLH), ("b_router", NE), ("eps", 1), ("conv_past", 8 * 3),
               ("bgate", 2), ("m0c", 1), ("w_router", KD * NE)):
    SMALL[_n] = (_at, _at + _w)
    _at += _w
NSMALL = _at
CONST = {}
_at = 0
for _n, _w in (("ident", P), ("ones", P), ("tri", P), ("blk", P), ("mask_s", 448), ("mask_i", 448), ("sel", MLH * P),
               ("iota", CAP)):
    CONST[_n] = (_at, _at + _w)
    _at += _w
NCONST = _at


class Chain:

    def __init__(self, eng, sem):
        self.eng, self.sem, self.n = eng, sem, 0

    def step(self, ins):
        ins.then_inc(self.sem, 1)
        self.n = self.n + 1

    def wait(self):
        self.eng.wait_ge(self.sem, self.n)

    def __call__(self, ins):
        self.step(ins)
        self.wait()


def build(nc, xT, small, const, b_exp, kcT, vc, c0, c0T, w_ada, w_in, w_out, w_gu, w_down,
          yT, koT, voT, convo, co, no, mo):
    ctx = ExitStack()
    with ctx:
        def sb(name, shape, dt=F32):
            return ctx.enter_context(nc.sbuf_tensor(name, shape, dt))

        def sem(name):
            return ctx.enter_context(nc.semaphore(name))

        ring = sb("ring", [P, SLOTS, 8, CHC])
        csb = sb("csb", [P, NCONST])
        ssb = sb("ssb", [P, NSMALL])
        x = sb("x", [P, KD, T])
        h = sb("h", [P, KD, T])
        wgate = sb("wgate", [P, KD, 8])
        tiny = sb("tiny", [P, 336])
        modrow = sb("modrow", [P, 4, P])
        WORK = 18760
        work = sb("work", [P, WORK])
        psum = ctx.enter_context(nc.psum_tensor("psum", [P, 8, 512], F32))
        bank = [psum[:, i, :] for i in range(8)]

        def K(name):
            return csb[:, CONST[name][0]:CONST[name][1]]

        def Sm(name):
            return ssb[:, SMALL[name][0]:SMALL[name][1]]

        ident, ones, tri, blk = K("ident"), K("ones"), K("tri"), K("blk")
        mask_s, mask_i = K("mask_s"), K("mask_i")
        iota_c = K("iota")
        iota_e = iota_c[:, 0:NE]
        sel = K("sel").rearrange("p (h n) -> p h n", h=MLH)
        wrout = Sm("w_router").rearrange("p (k e) -> p k e", k=KD)
        eps = Sm("eps")

        def region(start):
            at = [start]

            def take(*dims, dt=F32):
                n = int(np.prod(dims))
                cols = n if dt == F32 else n // 2
                v = work[:, at[0]:at[0] + cols]
                at[0] += cols
                assert at[0] <= WORK, at[0]
                if dt != F32:
                    v = v.bitcast(dt)
                if len(dims) > 1:
                    names = "abcd"[:len(dims)]
                    v = v.rearrange(f"p ({' '.join(names)}) -> p {' '.join(names)}", **dict(zip(names, dims)))
                return v
            return take, at

        take, at = region(0)
        q = take(4, T)
        k = take(4, 384)
        vT = take(4, T)
        kc = take(4, PAST)
        vpast = take(512)
        vtok = take(3, 512)
        end_sb = at[0]
        raw = take(8, RAWW)
        y = take(8, CONVW)
        mo_g = take(4, T)
        mix = take(8, T)
        mvT = mix[:, 4:8, :]
        scr = take(6, 512)
        take2, at2 = region(0)
        mq = take2(4, T)
        mk = take2(4, 384)
        mvtok = take2(3, 512)
        mktok = take2(3, 512)
        assert at2[0] <= end_sb
        sgy = raw.rearrange("p a b -> p (a b)")[:, 0:8 * CONVW].rearrange("p (a b) -> p a b", a=8)
        take3, at3 = region(end_sb + 8 * RAWW)
        C0 = take3(MLH, P)
        C0T = take3(MLH, P)
        Cout = take3(2, MLH, P)
        hh = take3(T)
        assert at3[0] <= end_sb + 8 * RAWW + 8 * CONVW
        sq = mix
        take4, _ = region(0)
        h2p = take4(3, 3, D, dt=BF16)
        xg = take4(KD, CAP)
        actT = take4(8, CAP)
        gc = take4(512)
        lc = take4(2, 512)
        sg = take4(512)
        otok = take4(2, 512)
        spread = take4(T)
        pick = take4(3, CAP, dt=BF16)
        wpick = take4(3, CAP)
        eh = take4(CAP)
        brow = take4(3 * D)
        acc = take4(8, T)
        res = take4(2, 512)
        act = res
        member = take4(3, NE)
        gate = take4(3, NE)
        rank = take4(3, NE)
        lg = take4(3, NE)

        tat = [0]

        def tn(*dims, dt=F32):
            n = int(np.prod(dims))
            v = tiny[:, tat[0]:tat[0] + n]
            tat[0] += n
            if dt != F32:
                v = v.bitcast(dt)
            if len(dims) > 1:
                names = "abcd"[:len(dims)]
                v = v.rearrange(f"p ({' '.join(names)}) -> p {' '.join(names)}", **dict(zip(names, dims)))
            return v

        cs = tn(KD, 2)
        mod = tn(48, 2)
        s1 = tn(KD, 2)
        s2 = tn(KD, 2)
        gqs = tn(1)
        gtok = tn(3, 8)
        acol = tn(3, MLH)
        nout = tn(2, MLH)
        mout = tn(2)
        top = tn(3, 8)
        topi = tn(3, 8, dt=U32)
        topf = tn(3, 8)
        negv = tn(3)
        rs4 = tn(3)
        cnt = tn(NE)
        cmax = tn(1)
        cmaxi = tn(1, dt=I32)
        cnti = tn(NE, dt=I32)
        rows = sb("rows", [P, 4, T])

        ld_small = sem("ld_small")
        ld_side = sem("ld_side")
        ld_bias = sem("ld_bias")
        ld_state = sem("ld_state")
        slot_full = [sem(f"slot_full{i}") for i in range(SLOTS)]
        v_chain, a_chain, g_chain = sem("v_chain"), sem("a_chain"), sem("g_chain")
        v_init = sem("v_init")
        csig = sem("csig")
        cs_ready = sem("cs_ready")
        xsq_ready = sem("xsq_ready")
        ss1_ps = sem("ss1_ps")
        rstd1_ready = sem("rstd1_ready")
        hs_ready = sem("hs_ready")
        h_ready = sem("h_ready")
        ada_used = sem("ada_used")
        mod1_ready = sem("mod1_ready")
        mod2_ready = sem("mod2_ready")
        proj_ps = sem("proj_ps")
        sq_ready = sem("sq_ready")
        proj_done = sem("proj_done")
        nss_ps = sem("nss_ps")
        nrs_ready = sem("nrs_ready")
        qk_ready = sem("qk_ready")
        vtr_ps = sem("vtr_ps")
        vtok_ready = sem("vtok_ready")
        gates_ps = sem("gates_ps")
        gtok_ready = sem("gtok_ready")
        grow_ps = sem("grow_ps")
        frow_ready = sem("frow_ready")
        flog_ready = sem("flog_ready")
        rows_ready = sem("rows_ready")
        conv_ready = sem("conv_ready")
        z_ps = sem("z_ps")
        l_ready = sem("l_ready")
        sp_ready = sem("sp_ready")
        spm_ready = sem("spm_ready")
        between_ps = sem("between_ps")
        t_ready = sem("t_ready")
        e_ready = sem("e_ready")
        a_ready = sem("a_ready")
        av_ps = sem("av_ps")
        av_done = sem("av_done")
        sgy_ready = sem("sgy_ready")
        mkq_ready = sem("mkq_ready")
        ktr_ps = sem("ktr_ps")
        mvtr_ps = sem("mvtr_ps")
        ktok_ready = sem("ktok_ready")
        mvtok_ready = sem("mvtok_ready")
        acol_ps = sem("acol_ps")
        acol_ready = sem("acol_ready")
        mb_ps = sem("mb_ps")
        mt_ps = sem("mt_ps")
        st_ps = sem("st_ps")
        wtmp_ready = sem("wtmp_ready")
        w_ready = sem("w_ready")
        s_ready = sem("s_ready")
        sm_ready = sem("sm_ready")
        qw_ready = sem("qw_ready")
        kw_ready = sem("kw_ready")
        num_ps = sem("num_ps")
        state_ps = sem("state_ps")
        hd_ready = sem("hd_ready")
        hsq_ready = sem("hsq_ready")
        hss_ps = sem("hss_ps")
        hrs_ready = sem("hrs_ready")
        mix_ready = sem("mix_ready")
        state_out = sem("state_out")
        xo_ps = sem("xo_ps")
        x1_ready = sem("x1_ready")
        x1sq_ready = sem("x1sq_ready")
        ss2_ps = sem("ss2_ps")
        rstd2_ready = sem("rstd2_ready")
        hs2_ready = sem("hs2_ready")
        h2_ready = sem("h2_ready")
        logit_ps = sem("logit_ps")
        top_ready = sem("top_ready")
        ex_ready = sem("ex_ready")
        member_ready = sem("member_ready")
        rank_ps = sem("rank_ps")
        cnt_ready = sem("cnt_ready")
        h2tr_ps = sem("h2tr_ps")
        hi_ready = sem("hi_ready")
        r_ready = sem("r_ready")
        mid_ready = sem("mid_ready")
        lo_ready = sem("lo_ready")
        rank_moved = sem("rank_moved")
        pick_ready = sem("pick_ready")
        gath_ps = sem("gath_ps")
        xg_ready = sem("xg_ready")
        atr_ps = sem("atr_ps")
        at_ready = sem("at_ready")
        eh_ready = sem("eh_ready")
        modrow_ps = sem("modrow_ps")
        modrow_ready = sem("modrow_ready")
        modt_ps = sem("modt_ps")
        gu_ps = sem("gu_ps")
        gc_ready = sem("gc_ready")
        lc_ready = sem("lc_ready")
        sg_ready = sem("sg_ready")
        gl_ready = sem("gl_ready")
        act_ready = sem("act_ready")
        dn_ps = sem("dn_ps")
        wpick_ready = sem("wpick_ready")
        otok_ready = sem("otok_ready")
        str_ps = sem("str_ps")
        spread_ready = sem("spread_ready")
        sc_ps = sem("sc_ps")
        acc_ready = sem("acc_ready")
        acc_closed = sem("acc_closed")
        y_ready = sem("y_ready")
        sb_stored = sem("sb_stored")
        conv_stored = sem("conv_stored")
        state_stored = sem("state_stored")
        y_stored = sem("y_stored")

        def tok(tt):
            return slice(TILES[tt][0], TILES[tt][0] + TILES[tt][1])

        SEQ = ((slice(0, TP), 0), (slice(TP, T), 1))

        def expert_chunks(e):
            gu = w_gu.rearrange("o e (k p) n -> (o e) p k n", p=P)
            dn = w_down.rearrange("o e (k p) n -> (o e) p k n", p=P)
            return [gu[e, :, :, 0:CHC], gu[e, :, :, D:D + CHC], gu[e, :, :, CHC:D], gu[e, :, :, D + CHC:2 * D],
                    dn[e, :, :, 0:CHC], dn[e, :, :, CHC:D]]

        def expert_turn(j):
            return j, (PRE + j) // SLOTS

        def used_before(n):
            if n < ADA1:
                return ada_used, n + 1
            n -= ADA1
            if n < SBP + MLP:
                return proj_ps, 4 * n + 4
            n -= SBP + MLP
            if n < ADA2:
                return ada_used, ADA1 + n + 1
            return xo_ps, 4 * (n - ADA2) + 4

        def used_expert(j, turn):
            if j < 4:
                return gu_ps, turn * 2 + (j // 2 + 1)
            return dn_ps, turn * 2 + (j - 4 + 1)

        def passes(eng, start, expert, finish):
            eng.wait_ge(cnt_ready, 1)
            start(0, 0, 0)
            expert(0, 0, 0, True, False)
            with eng.Fori(1, NE - 1) as e:
                expert(e, e, 0, False, False)
            expert(NE - 1, NE - 1, 0, False, True)
            finish(NE - 1, 0)
            most = eng.value_load(cmaxi[0:1, 0:1], min_val=0, max_val=T)
            with eng.Fori(1, PASSES) as b:
                with eng.If(most > b * CAP):
                    start(b * NE, 0, b)
                    expert(b * NE, 0, b, True, False)
                    with eng.Fori(1, NE - 1) as e:
                        expert(b * NE + e, e, b, False, False)
                    expert(b * NE + (NE - 1), NE - 1, b, False, True)
                    finish(b * NE + (NE - 1), b)

        def count(eng, e):
            return eng.value_load(cnti[0:1, bass.ds(e, 1)], min_val=0, max_val=T)

        def by_size(eng, n, b, body):
            with eng.If(n > b * CAP + CAP // 2):
                body(1)
            with eng.Else():
                with eng.If(n > b * CAP + CAP // 4):
                    body(2)
                with eng.Else():
                    body(4)

        block = ctx.enter_context(nc.Block())

        @block.sync
        def _(sp):
            ada = w_ada.rearrange("o (k p) n -> (o p) k n", p=P)
            win = w_in.rearrange("o (k p) n -> (o p) k n", p=P)
            wo = w_out.rearrange("o (k p) n -> (o p) k n", p=P)
            pre = [ada[:, :, j * CHC:(j + 1) * CHC] for j in range(ADA1)]
            pre += [win[:, :, j * CHC:(j + 1) * CHC] for j in range(SBP + MLP - 1)]
            pre += [win[:, :, 3080:3080 + CHC]]
            pre += [ada[:, :, j * CHC:(j + 1) * CHC] for j in range(ADA1, ADA1 + ADA2)]
            pre += [wo[:, :, j * CHC:(j + 1) * CHC] for j in range(WO)]
            assert len(pre) == PRE
            for n, src in enumerate(pre):
                if n >= SLOTS:
                    sp.wait_ge(*used_before(n - SLOTS))
                slot = (n + SHIFT) % SLOTS
                sp.dma_start(ring[:, slot], src).then_inc(slot_full[slot], 16)

            for j, src in enumerate(expert_chunks(0)):
                sp.wait_ge(*used_before(PRE + j - SLOTS))
                sp.dma_start(ring[:, expert_turn(j)[0]], src).then_inc(slot_full[expert_turn(j)[0]], 16)

            def load_expert(e, turn):
                for j, src in enumerate(expert_chunks(e)):
                    sp.wait_ge(*used_expert(j, turn - 1))
                    sp.dma_start(ring[:, expert_turn(j)[0]], src).then_inc(slot_full[expert_turn(j)[0]], 16)

            with sp.Fori(1, NE) as e:
                load_expert(e, e)
            sp.wait_ge(cnt_ready, 1)
            most = sp.value_load(cmaxi[0:1, 0:1], min_val=0, max_val=T)
            with sp.Fori(1, PASSES) as b:
                with sp.If(most > b * CAP):
                    with sp.Fori(0, NE) as e:
                        load_expert(e, b * NE + e)
            yv = yT.rearrange("(k p) t -> p k t", p=P)
            for c in range(4):
                sp.wait_ge(y_ready, 4 * (c + 1))
                sp.dma_start(yv[:, 2 * c:2 * c + 2, :], h[:, 2 * c:2 * c + 2, :]).then_inc(y_stored, 16)
            sp.wait_ge(y_stored, 16 * 4)
            sp.wait_ge(sb_stored, 16 * 2)
            sp.wait_ge(conv_stored, 16 * 2)
            sp.wait_ge(state_stored, 16 * 3)

        @block.tensor
        def _(pe):
            mm = nc.tensor.matmul
            used = [0]

            def chunk():
                n = used[0]
                slot = (n + SHIFT) % SLOTS
                pe.wait_ge(slot_full[slot], 16 * (n // SLOTS + 1))
                used[0] += 1
                return ring[:, slot]

            pe.wait_ge(ld_small, 16 * 4)
            pe.wait_ge(xsq_ready, 1)
            for kk in range(KD):
                last = mm(bank[7][:, 0:T], ones, sq[:, kk, :], start=kk == 0, stop=kk == KD - 1)
            last.then_inc(ss1_ps, 1)
            pe.wait_ge(cs_ready, 1)

            def ada(bk):
                w = chunk()
                c = (used[0] - 1) % 4 if used[0] <= ADA1 else (used[0] - 1 - ADA1 - SBP - MLP) % 4
                for kk in range(KD):
                    for g in range(4):
                        last = mm(bank[bk][32 * g:32 * g + 2, c * P:(c + 1) * P], cs[:, kk, :], w[:, kk, g * P:(g + 1) * P],
                                  start=kk == 0, stop=kk == KD - 1)
                last.then_inc(ada_used, 1)

            def ada_turn(batch, bk):
                pe.wait_ge(modrow_ready, 4 * (batch + 1))
                for c in range(4):
                    last = nc.tensor.transpose(bank[bk][:, c * P:(c + 1) * P], modrow[:, c, :], ident)
                last.then_inc(modt_ps, 1)

            for c in range(4):
                ada(2)
            ada_turn(0, 3)
            pe.wait_ge(h_ready, 16)
            tile = [0]
            hold = [None]

            def proj():
                t = tile[0]
                if t % 4 == 0:
                    hold[0] = chunk()
                w = hold[0]
                if t >= 2:
                    pe.wait_ge(*((sq_ready, t - 1) if t < 10 else (proj_done, t - 9)))
                for kk in range(KD):
                    last = mm(bank[t % 2][:, 0:T], w[:, kk, (t % 4) * P:(t % 4 + 1) * P], h[:, kk, :], start=kk == 0, stop=kk == KD - 1)
                last.then_inc(proj_ps, 1)
                tile[0] += 1

            def nss(i):
                if i >= 2:
                    pe.wait_ge(nrs_ready, i - 1)
                pe.wait_ge(sq_ready, i + 1)
                mm(bank[6 + i % 2][:, 0:T], blk, scr[:, i % 2, 0:T], start=True, stop=True).then_inc(nss_ps, 1)

            for t in range(8):
                proj()
                if t >= 1:
                    nss(t - 1)
            proj()
            nss(7)
            for t in range(3):
                proj()
            for tt, (t0, n) in enumerate(TILES):
                for kk in range(KD):
                    last = mm(bank[5][0:n, tt * 8:tt * 8 + 8], h[:, kk, t0:t0 + n], wgate[:, kk, :], start=kk == 0, stop=kk == KD - 1)
            last.then_inc(gates_ps, 1)
            pe.wait_ge(proj_done, 4)
            pe.wait_ge(mod1_ready, 1)
            for tt, (t0, n) in enumerate(TILES):
                for c in range(4):
                    last = nc.tensor.transpose(bank[2 + tt][0:n, c * P:(c + 1) * P], vT[:, c, t0:t0 + n], ident)
                last.then_inc(vtr_ps, 1)
            pe.wait_ge(gtok_ready, 1)
            pe.wait_ge(nrs_ready, 8)
            for g in range(2):
                for tt, (t0, n) in enumerate(TILES):
                    last = nc.tensor.transpose(bank[6 + g][0:MLH, t0:t0 + n], gtok[0:n, tt, g * MLH:(g + 1) * MLH], ident[0:n, 0:n])
            last.then_inc(grow_ps, 1)
            pe.wait_ge(qk_ready, 8)
            pe.wait_ge(vtok_ready, 3)
            pe.wait_ge(ld_side, 16 * 2)

            def z_of(hd):
                r0 = 64 * (hd % 2)
                r = slice(r0, r0 + 64)
                c = hd // 2
                zb = bank[2 + hd % 2]
                if hd >= 2:
                    pe.wait_ge(t_ready, hd - 1)
                mm(zb[:, AC], k[r, c, 0:128], q[r, c, 0:256], start=True, stop=True)
                mm(zb[:, B], k[r, c, 128:256], q[r, c, 128:256], start=True, stop=True)
                mm(zb[:, E], k[r, c, 256:384], q[r, c, 256:320], start=True, stop=True)
                mm(zb[:, DP], kc[r, c, :], q[r, c, 256:320], start=True, stop=True).then_inc(z_ps, 1)

            def between_of(hd):
                pe.wait_ge(spm_ready, hd + 1)
                if hd >= 2:
                    pe.wait_ge(t_ready, hd - 1)
                sp_ = scr[:, 3 * (hd % 2) + 1, :]
                bb = bank[4 + hd % 2]
                mm(bb[:, :], tri, sp_, start=True, stop=False)
                mm(bb[:, C], ones, sp_[:, B], start=False, stop=False)
                mm(bb[:, DP], ones, sp_[:, E], start=False, stop=True).then_inc(between_ps, 1)

            def av_of(hd):
                pe.wait_ge(a_ready, hd + 1)
                if hd % 2 == 0 and hd:
                    pe.wait_ge(av_done, hd // 2)
                if hd == 0:
                    pe.wait_ge(frow_ready, 1)
                r = slice(64 * (hd % 2), 64 * (hd % 2) + 64)
                vc_ = slice(hd * 64, hd * 64 + 64)
                a_ = scr[:, 3 * (hd % 2) + 2, :]
                ob = bank[6]
                mm(ob[r, 0:128], vtok[:, 0, vc_], a_[:, A], start=True, stop=True)
                mm(ob[r, 128:256], vtok[:, 0, vc_], a_[:, C], start=True, stop=False)
                mm(ob[r, 128:256], vtok[:, 1, vc_], a_[:, B], start=False, stop=True)
                mm(ob[r, 256:320], vpast[:, vc_], a_[:, DP], start=True, stop=False)
                mm(ob[r, 256:320], vtok[0:64, 2, vc_], a_[0:64, E], start=False, stop=True).then_inc(av_ps, 1)

            for i in range(SBH + 2):
                if 1 <= i < SBH + 1:
                    between_of(i - 1)
                if i >= 2:
                    av_of(i - 2)
                if i < SBH:
                    z_of(i)
                    proj()
                    proj()

            pe.wait_ge(mkq_ready, 1)
            pe.wait_ge(proj_done, 20)
            pe.wait_ge(t_ready, 8)
            pe.wait_ge(av_done, 4)
            for tt, (t0, n) in enumerate(TILES):
                for c in range(4):
                    last = nc.tensor.transpose(bank[tt][0:n, c * P:(c + 1) * P], mk[:, c, t0:t0 + n], ident)
                last.then_inc(ktr_ps, 1)
            for tt, (t0, n) in enumerate(TILES):
                for c in range(4):
                    last = nc.tensor.transpose(bank[3 + tt][0:n, c * P:(c + 1) * P], mvT[:, c, t0:t0 + n], ident)
                last.then_inc(mvtr_ps, 1)
            pe.wait_ge(rows_ready, 1)
            for tt, (t0, n) in enumerate(TILES):
                last = nc.tensor.transpose(bank[6][0:n, tt * 4:tt * 4 + 4], rows[0:MLH, 0, t0:t0 + n], ident[0:MLH, 0:MLH])
            last.then_inc(acol_ps, 1)
            pe.wait_ge(ktok_ready, 3)
            pe.wait_ge(mvtok_ready, 3)
            pe.wait_ge(acol_ready, 1)
            pe.wait_ge(ld_state, 16 * 2)

            def ml_scores(i):
                if i:
                    pe.wait_ge(w_ready, i)
                mm_ = mm(bank[3][:, 0:T], sel[0:MLH, i, :], rows[0:MLH, 1, :], start=True, stop=True)
                mm_.then_inc(mb_ps, 1)
                mm(bank[4][:, 0:T], sel[0:MLH, i, :], rows[0:MLH, 3, :], start=True, stop=True).then_inc(mt_ps, 1)
                if i:
                    pe.wait_ge(s_ready, i)
                mm(bank[2][:, AC], mk[:, i, 0:128], mq[:, i, 0:256], start=True, stop=True)
                mm(bank[2][:, B], mk[:, i, 128:256], mq[:, i, 128:256], start=True, stop=True)
                mm(bank[2][:, E], mk[:, i, 256:384], mq[:, i, 256:320], start=True, stop=True).then_inc(st_ps, 1)

            def ml_values(i):
                S_ = scr[:, 1, :]
                qw = scr[:, 3, 0:64]
                nb = scr[:, 3, 64:192]
                kw = scr[:, 2, 0:384].rearrange("p (a b) -> p a b", a=3)
                pe.wait_ge(sm_ready, i + 1)
                pe.wait_ge(qw_ready, i + 1)
                hc = slice(i * P, (i + 1) * P)
                if i:
                    pe.wait_ge(hd_ready, i)
                for bk, l0, l1, l2, li in ((5, mvtok[:, 0, hc], mvtok[:, 1, hc], mvtok[0:64, 2, hc], C0T[:, i, :]),
                                           (6, ones, ones, ones[0:64, :], nb)):
                    mm(bank[bk][:, 0:256], l0, S_[:, AC], start=True, stop=False)
                    mm(bank[bk][:, 128:256], l1, S_[:, B], start=False, stop=True)
                    mm(bank[bk][:, 256:320], l2, S_[0:64, E], start=True, stop=False)
                    last = mm(bank[bk][:, 256:320], li, qw, start=False, stop=True)
                last.then_inc(num_ps, 1)
                pe.wait_ge(kw_ready, i + 1)
                if i:
                    pe.wait_ge(state_out, i)
                sbk = bank[1]
                mm(sbk[:, 0:128], mvtok[:, 0, hc], kw[:, 0, :], start=True, stop=False)
                mm(sbk[:, 0:128], mvtok[:, 1, hc], kw[:, 1, :], start=False, stop=True)
                mm(sbk[:, 128:256], mvtok[0:64, 2, hc], kw[0:64, 2, :], start=True, stop=True)
                mm(sbk[:, 256:257], kw[:, 0, :], ones[:, 0:1], start=True, stop=False)
                mm(sbk[:, 256:257], kw[:, 1, :], ones[:, 0:1], start=False, stop=True)
                mm(sbk[:, 257:258], kw[0:64, 2, :], ones[0:64, 0:1], start=True, stop=True).then_inc(state_ps, 1)

            def ml_norm(i):
                pe.wait_ge(hsq_ready, i + 1)
                if i:
                    pe.wait_ge(hrs_ready, i)
                mm(bank[7][:, 0:T], ones, scr[:, 5, 0:T], start=True, stop=True).then_inc(hss_ps, 1)

            for i in range(MLH):
                if i == 2:
                    pe.wait_ge(mod2_ready, 1)
                ml_scores(i)
                if i == 2:
                    pe.wait_ge(modrow_ready, 8)
                ada(0)
                if i:
                    ml_norm(i - 1)
                ml_values(i)
                ada(0)
                if i == 1:
                    ada_turn(1, 2)
            ml_norm(MLH - 1)
            ada_turn(2, 2)

            pe.wait_ge(mix_ready, 4)
            for t in range(8):
                if t % 4 == 0:
                    hold[0] = chunk()
                w = hold[0]
                if t >= 2:
                    pe.wait_ge(x1_ready, 2 * t - 2)
                for kk in range(KD):
                    last = mm(bank[4 + t % 2][:, 0:T], w[:, kk, (t % 4) * P:(t % 4 + 1) * P], mix[:, kk, :], start=kk == 0, stop=kk == KD - 1)
                last.then_inc(xo_ps, 1)
            for kk in range(KD):
                pe.wait_ge(x1sq_ready, kk + 1)
                last = mm(bank[7][:, 0:T], ones, h[:, kk, :], start=kk == 0, stop=kk == KD - 1)
            last.then_inc(ss2_ps, 1)
            assert used[0] == PRE

            pe.wait_ge(h2_ready, 16)
            for tt, (t0, n) in enumerate(TILES):
                for kk in range(KD):
                    last = mm(bank[6][0:n, tt * NE:(tt + 1) * NE], h[:, kk, t0:t0 + n], wrout[:, kk, :], start=kk == 0, stop=kk == KD - 1)
            last.then_inc(logit_ps, 1)
            for i in range(6):
                tt, half = i // 2, i % 2
                t0, n = TILES[tt]
                if i >= 2:
                    pe.wait_ge(r_ready, i - 1)
                for c in range(4):
                    last = nc.tensor.transpose(bank[i % 2][0:n, c * P:(c + 1) * P], h[:, half * 4 + c, t0:t0 + n], ident)
                last.then_inc(h2tr_ps, 1)
            pe.wait_ge(member_ready, 1)
            rb = bank[5]
            strict = mask_s[:, A]
            for tt in range(3):
                for u in range(tt + 1):
                    mm(rb[:, tt * NE:(tt + 1) * NE], strict if u == tt else ones, member[:, u, :], start=u == 0, stop=u == tt)
            for u in range(3):
                last = mm(rb[:, 96:128], ones, member[:, u, :], start=u == 0, stop=u == 2)
            last.then_inc(rank_ps, 1)
            pe.wait_ge(lo_ready, 6)

            X, U, R, DN = 0, 2, 4, 6

            def gather(turn, groups):
                n = CAP // groups
                per = min(8, 512 // n)
                for c in range(8):
                    for tt, (t0, nt) in enumerate(TILES):
                        for part in range(3):
                            last = mm(psum[:, X + c // per, c % per * n:(c % per + 1) * n], h2p[0:nt, part, tt, c * P:(c + 1) * P],
                                      pick[0:nt, tt, 0:n], start=tt == 0 and part == 0, stop=tt == 2 and part == 2)
                last.then_inc(gath_ps, 1)

            def weights(j, turn):
                slot, rounds = expert_turn(j)
                pe.wait_ge(slot_full[slot], (turn + (rounds + 1)) * 16)
                return ring[:, slot]

            def gate_up(i, turn, groups):
                m = CAP // groups
                parts = max(groups, 2)
                n = CHC // parts
                weights(2 * i, turn)
                weights(2 * i + 1, turn)
                both = ring[:, 2 * i:2 * i + 2]
                biases = brow[0:NE, 0:2 * D].rearrange("p (s n) -> p s n", s=2)
                for kk in range(KD + 1):
                    if kk == KD - 1 and i == 0:
                        pe.wait_ge(eh_ready, turn + 1)
                    for g in range(parts):
                        o = psum[:, U + g, :] if groups == 1 else psum[m * g:m * (g + 1), U + i, 0:2 * n]
                        if kk < KD:
                            l, r = xg[:, kk, 0:m], both[:, :, kk, g * n:(g + 1) * n]
                        else:
                            b0 = i * CHC + g * n
                            l, r = eh[0:NE, 0:m], biases[:, :, b0:b0 + n]
                        last = mm(o.rearrange("p (s n) -> p s n", s=2), l, r, start=kk == 0, stop=kk == KD)
                last.then_inc(gu_ps, 1)

            def turn_act(i, turn, groups):
                pe.wait_ge(act_ready, turn * 2 + (i + 1))
                for c in range(4 // groups):
                    last = nc.tensor.transpose(bank[R + i][:, c * P:(c + 1) * P], act[:, i, c * P:(c + 1) * P], ident)
                last.then_inc(atr_ps, 1)

            def down(i, turn, groups):
                m, n = CAP // groups, CHC // groups
                w = weights(4 + i, turn)
                pe.wait_ge(at_ready, turn * 2 + 2)
                for kk in range(9):
                    for g in range(groups):
                        if kk < 8:
                            l, r = actT[:, kk, 0:m], w[:, kk, g * n:(g + 1) * n]
                        else:
                            b0 = 2 * D + i * CHC + g * n
                            l, r = eh[0:NE, 0:m], brow[0:NE, b0:b0 + n]
                        last = mm(bank[DN + i][m * g:m * (g + 1), 0:n], l, r, start=kk == 0, stop=kk == 8)
                last.then_inc(dn_ps, 1)

            def turn_pick(turn):
                for tt, (t0, n) in enumerate(TILES):
                    last = nc.tensor.transpose(bank[X + 1][0:CAP, t0:t0 + n], wpick[0:n, tt, :], ident[0:n, 0:n])
                last.then_inc(str_ps, 1)

            def scatter(i, turn, groups):
                m = CAP // groups
                for c in range(2):
                    if i:
                        pe.wait_ge(acc_ready, turn * 8 + (2 * c + 3))
                    for hf in range(2):
                        f = 2 * hf + c
                        g = f * groups // 4
                        c0_ = f * P - g * (CHC // groups)
                        rows_ = slice(m * g, m * (g + 1))
                        mm(bank[R + 2 * c + hf][:, 0:T], otok[rows_, i, c0_:c0_ + P], spread[rows_, :],
                           start=True, stop=True).then_inc(sc_ps, 1)

            def start(turn, e, b):
                n = count(pe, e)
                pe.wait_ge(pick_ready, turn * 3 + 3)
                if not isinstance(turn, int):
                    pe.wait_ge(xg_ready, turn)
                    pe.wait_ge(spread_ready, turn)
                by_size(pe, n, b, lambda groups: gather(turn, groups))

            def spread_out(i, turn, n, b):
                if i == 0:
                    pe.wait_ge(otok_ready, turn * 2 + 2)
                    pe.wait_ge(spread_ready, turn + 1)
                by_size(pe, n, b, lambda groups: scatter(i, turn, groups))

            def expert(turn, e, b, begins, ends):
                n = count(pe, e)
                before = None if begins else count(pe, e - 1)
                after = None if ends else count(pe, e + 1)
                pe.wait_ge(xg_ready, turn + 1)
                by_size(pe, n, b, lambda groups: gate_up(0, turn, groups))
                if not begins:
                    spread_out(0, turn - 1, before, b)

                def second(groups):
                    if groups == 1:
                        pe.wait_ge(lc_ready, turn * 2 + 1)
                    gate_up(1, turn, groups)
                by_size(pe, n, b, second)
                if not begins:
                    spread_out(1, turn - 1, before, b)
                if not ends:
                    pe.wait_ge(pick_ready, turn * 3 + 6)
                    if not isinstance(turn, int) or turn:
                        pe.wait_ge(spread_ready, turn)
                    by_size(pe, after, b, lambda groups: gather(turn + 1, groups))
                pe.wait_ge(acc_ready, turn * 8 + 1)

                def last_part(groups):
                    for i in range(2):
                        turn_act(i, turn, groups)
                    for i in range(2):
                        down(i, turn, groups)
                by_size(pe, n, b, last_part)
                pe.wait_ge(wpick_ready, turn * 3 + 3)
                if not ends:
                    pe.wait_ge(xg_ready, turn + 2)
                turn_pick(turn)

            def finish(turn, b):
                n = count(pe, NE - 1)
                spread_out(0, turn, n, b)
                spread_out(1, turn, n, b)

            pe.wait_ge(ld_bias, 16)
            passes(pe, start, expert, finish)

        @block.scalar
        def _(act_):
            chain = Chain(act_, a_chain)
            fn = nc.scalar.activation
            a_one = ones[:, 0:1]

            def copy(out, in_):
                return fn(out, in_, ACT.Copy)

            for dst, src in ((ssb[:], small), (csb[:], const), (x[:], xT.rearrange("(k p) t -> p k t", p=P)),
                             (wgate[:], w_in.rearrange("o (k p) n -> (o p) k n", p=P)[:, :, 3072:3080])):
                act_.dma_start(dst, src).then_inc(ld_small, 16)
            for dst, src in ((kc, kcT.rearrange("(c p) n -> p c n", p=P)), (vpast, vc)):
                act_.dma_start(dst, src).then_inc(ld_side, 16)
            act_.wait_ge(ld_small, 16 * 4)
            c_in = Sm("cT").rearrange("p (k s) -> p k s", k=KD)
            fn(cs, c_in, ACT.Sigmoid).then_inc(csig, 1)
            fn(sq, x[:], ACT.Square).then_inc(xsq_ready, 1)

            def rstd(out, ps, n, ready):
                chain(fn(out, ps, ACT.Ln, bias=eps, scale=1.0 / n))
                fn(out, out, ACT.Exp, scale=-0.5).then_inc(ready, 1)

            def mod_rows(batch, bk):
                act_.wait_ge(ada_used, 4 * (batch + 1))
                if batch:
                    act_.wait_ge(modt_ps, batch)
                for g in range(4):
                    r = slice(32 * g, 32 * g + 2)
                    copy(modrow[r].rearrange("p c n -> p (c n)"), bank[bk][r, :]).then_inc(modrow_ready, 1)

            act_.wait_ge(v_init, 4)
            act_.wait_ge(ss1_ps, 1)
            rstd(scr[:, 2, 0:T], bank[7][:, 0:T], D, rstd1_ready)
            mod_rows(0, 2)
            act_.wait_ge(mod1_ready, 1)
            for kk in range(KD):
                act_.wait_ge(hs_ready, 2 * kk + 2)
                for cols, sq_ in SEQ:
                    fn(h[:, kk, cols], h[:, kk, cols], ACT.Identity, bias=mod[:, kk, sq_:sq_ + 1]).then_inc(h_ready, 1)

            dst = [q[:, c, :] for c in range(4)] + [k[:, c, 0:T] for c in range(4)] + [vT[:, c, :] for c in range(4)]
            dst += [raw[:, c, :] for c in range(8)] + [mvT[:, c, :] for c in range(4)] + [mo_g[:, c, :] for c in range(4)]

            def proj_out(t):
                act_.wait_ge(proj_ps, t + 1)
                pb = bank[t % 2]
                if t < 8:
                    copy(dst[t], pb[:, 0:T])
                    if t >= 2:
                        act_.wait_ge(nss_ps, t - 1)
                    fn(scr[:, t % 2, 0:T], pb[:, 0:T], ACT.Square).then_inc(sq_ready, 1)
                elif 12 <= t < 20:
                    copy(dst[t][:, CW - 1:CW - 1 + TP], pb[:, 0:TP])
                    copy(dst[t][:, CS + CW - 1:RAWW], pb[:, TP:T]).then_inc(proj_done, 1)
                else:
                    copy(dst[t], pb[:, 0:T]).then_inc(proj_done, 1)

            def nrs(i):
                act_.wait_ge(nss_ps, i + 1)
                if i >= 2:
                    act_.wait_ge(qk_ready, i - 1)
                rstd(scr[:, 2 + i % 2, 0:T], bank[6 + i % 2][:, 0:T], SBD, nrs_ready)

            act_.wait_ge(v_init, 4)
            for t in range(12):
                proj_out(t)
                if 1 <= t < 9:
                    nrs(t - 1)
            act_.wait_ge(proj_done, 4)
            act_.dma_start(voT.rearrange("(c p) t -> p c t", p=P), vT).then_inc(sb_stored, 16)
            act_.wait_ge(qk_ready, 8)
            act_.dma_start(koT.rearrange("(c p) t -> p c t", p=P), k[:, :, 0:T]).then_inc(sb_stored, 16)

            act_.wait_ge(frow_ready, 1)
            chain(fn(rows[0:MLH, 2, :], rows[0:MLH, 1, :], ACT.Abs))
            chain(fn(rows[0:MLH, 2, :], rows[0:MLH, 2, :], ACT.Exp, scale=-1.0))
            fn(rows[0:MLH, 2, :], rows[0:MLH, 2, :], ACT.Ln, bias=a_one[0:MLH]).then_inc(flog_ready, 1)

            for i in range(SBH + 1):
                if i >= 1:
                    act_.wait_ge(t_ready, i)
                    tt_ = scr[:, 3 * ((i - 1) % 2) + 2, :]
                    fn(tt_, tt_, ACT.Exp).then_inc(e_ready, 1)
                if i < SBH:
                    act_.wait_ge(z_ps, i + 1)
                    l = scr[:, 3 * (i % 2), :]
                    chain(fn(l, bank[2 + i % 2][:, :], ACT.Abs))
                    chain(fn(l, l, ACT.Exp, scale=-1.0))
                    fn(l, l, ACT.Ln, bias=a_one).then_inc(l_ready, 1)
                    proj_out(12 + 2 * i)
                    proj_out(13 + 2 * i)

            act_.wait_ge(proj_done, 20)
            cv = convo.rearrange("(c p) s w -> p c s w", p=P)
            with nc.allow_non_contiguous_dma(reason="three columns of each row"):
                act_.dma_start(cv[:, :, 0, :], raw[:, :, TP:TP + 3]).then_inc(conv_stored, 16)
                act_.dma_start(cv[:, :, 1, :], raw[:, :, RAWW - 3:RAWW]).then_inc(conv_stored, 16)
            act_.wait_ge(conv_ready, 8)
            act_.wait_ge(conv_stored, 32)
            fn(sgy, y, ACT.Sigmoid)
            fn(mo_g, mo_g, ACT.Sigmoid).then_inc(sgy_ready, 1)
            act_.wait_ge(mkq_ready, 1)
            act_.dma_start(C0, c0).then_inc(ld_state, 16)
            act_.dma_start(C0T, c0T).then_inc(ld_state, 16)
            act_.wait_ge(rows_ready, 1)
            with nc.allow_non_contiguous_dma(reason="one element per head"):
                act_.dma_start(mo, rows[0:MLH, 3, TP - 1:T:TS]).then_inc(state_stored, 16)
            for tt, (t0, n) in enumerate(TILES):
                act_.wait_ge(mvtr_ps, tt + 1)
                copy(mvtok[0:n, tt, :], bank[3 + tt][0:n, :]).then_inc(mvtok_ready, 1)

            def hrs(i):
                act_.wait_ge(hss_ps, i + 1)
                rstd(scr[:, 5, 0:T], bank[7][:, 0:T], MLD, hrs_ready)

            for i in range(MLH):
                act_.wait_ge(mt_ps, i + 1)
                fn(scr[:, 4, 0:T], bank[4][:, 0:T], ACT.Exp, scale=-1.0)
                act_.wait_ge(wtmp_ready, i + 1)
                fn(scr[:, 0, ACBE], scr[:, 0, ACBE], ACT.Exp, scale=-1.0)
                fn(scr[:, 3, 192:256], bank[3][:, TP:T], ACT.Exp, bias=Sm("m0b")[:, i:i + 1], scale=-1.0).then_inc(w_ready, 1)
                if i:
                    hrs(i - 1)
                act_.wait_ge(hd_ready, i + 1)
                fn(scr[:, 5, 0:T], hh, ACT.Square).then_inc(hsq_ready, 1)
                if i == 1:
                    mod_rows(1, 0)
            hrs(MLH - 1)
            mod_rows(2, 0)
            act_.wait_ge(state_out, MLH)
            act_.dma_start(co.rearrange("s h v k -> v (s h) k"), Cout.rearrange("p s h k -> p (s h) k")).then_inc(state_stored, 16)
            act_.dma_start(no, nout.rearrange("p s h -> p (s h)")).then_inc(state_stored, 16)

            for kk in range(KD):
                act_.wait_ge(x1_ready, 2 * kk + 2)
                fn(h[:, kk, :], x[:, kk, :], ACT.Square).then_inc(x1sq_ready, 1)
            act_.wait_ge(state_stored, 16 * 3)
            act_.dma_start(brow[0:NE, :], b_exp).then_inc(ld_bias, 16)
            act_.wait_ge(ss2_ps, 1)
            rstd(scr[:, 2, 0:T], bank[7][:, 0:T], D, rstd2_ready)
            act_.wait_ge(mod2_ready, 2)
            for kk in range(KD):
                act_.wait_ge(hs2_ready, 2 * kk + 2)
                for cols, sq_ in SEQ:
                    fn(h[:, kk, cols], h[:, kk, cols], ACT.Identity, bias=mod[:, 24 + kk, sq_:sq_ + 1]).then_inc(h2_ready, 1)
            act_.wait_ge(top_ready, 1)
            for tt in range(3):
                fn(gate[:, tt, :], lg[:, tt, :], ACT.Exp, bias=negv[:, tt:tt + 1]).then_inc(ex_ready, 1)
            for i in range(6):
                tt, half = i // 2, i % 2
                n = TILES[tt][1]
                hc = slice(half * 512, half * 512 + 512)
                act_.wait_ge(h2tr_ps, i + 1)
                copy(h2p[0:n, 0, tt, hc], bank[i % 2][0:n, :]).then_inc(hi_ready, 1)
                act_.wait_ge(r_ready, i + 1)
                copy(h2p[0:n, 1, tt, hc], res[0:n, i % 2, :]).then_inc(mid_ready, 1)

            def gathered(turn, groups):
                act_.wait_ge(gath_ps, turn + 1)
                if groups == 1:
                    last = copy(xg.rearrange("p (b c) n -> p b (c n)", b=2), psum[:, 0:2, :])
                else:
                    m = CAP // groups
                    last = copy(xg[:, :, 0:m], bank[0][:, 0:8 * m].rearrange("p (c n) -> p c n", c=8))
                last.then_inc(xg_ready, 1)

            def start(turn, e, b):
                by_size(act_, count(act_, e), b, lambda groups: gathered(turn, groups))

            def sigmoids(turn, groups):
                n = CHC // groups
                for i in range(2):
                    act_.wait_ge(gc_ready, turn * 2 + (i + 1))
                    fn(sg[:, 0:n], gc[:, 0:n], ACT.Sigmoid, scale=SWIGLU_ALPHA).then_inc(sg_ready, 1)

            def evacuate(turn, groups):
                m = CAP // groups
                for i in range(2):
                    act_.wait_ge(atr_ps, turn * 2 + (i + 1))
                    o = actT[:, 4 * i:4 * i + 4, 0:m].rearrange("p (g c) n -> p c g n", g=groups)
                    t_ = bank[4 + i][:, 0:CHC // groups].rearrange("p (c g n) -> p c g n", g=groups, n=m)
                    if groups == 1:
                        o, t_ = o[:, :, 0, :], t_[:, :, 0, :]
                    elif groups == 4:
                        o, t_ = o[:, 0, :, :], t_[:, 0, :, :]
                    copy(o, t_).then_inc(at_ready, 1)
                for i in range(2):
                    act_.wait_ge(dn_ps, turn * 2 + (i + 1))
                    n = CHC // groups
                    copy(otok[:, i, 0:n], bank[6 + i][:, 0:n]).then_inc(otok_ready, 1)

            def expert(turn, e, b, begins, ends):
                n = count(act_, e)
                after = None if ends else count(act_, e + 1)
                by_size(act_, n, b, lambda groups: sigmoids(turn, groups))
                if not ends:
                    by_size(act_, after, b, lambda groups: gathered(turn + 1, groups))
                by_size(act_, n, b, lambda groups: evacuate(turn, groups))
                act_.wait_ge(str_ps, turn + 1)
                copy(spread, bank[1][:, 0:T]).then_inc(spread_ready, 1)

            passes(act_, start, expert, lambda turn, b: None)

        @block.vector
        def _(v):
            chain = Chain(v, v_chain)
            ts, tt_, stt, cp = nc.vector.tensor_scalar, nc.vector.tensor_tensor, nc.vector.scalar_tensor_tensor, nc.vector.tensor_copy
            v.wait_ge(ld_small, 16 * 4)
            nc.vector.memset(k[:, :, T:384], 0.0).then_inc(v_init, 1)
            nc.vector.memset(raw[:, :, 0:CW - 1], 0.0).then_inc(v_init, 1)
            cp(raw[:, :, CW - 1 + TP:CS + CW - 1], Sm("conv_past").rearrange("p (c w) -> p c w", c=8)).then_inc(v_init, 1)
            chain.step(ts(gqs, Sm("gq"), SBD ** -0.5, None, ALU.mult))
            nc.vector.memset(acol[64:128, 2, :], 0.0)
            v.wait_ge(csig, 1)
            tt_(cs, Sm("cT").rearrange("p (k s) -> p k s", k=KD), cs, ALU.mult).then_inc(cs_ready, 1)

            nc.vector.memset(modrow[:], 0.0).then_inc(v_init, 1)

            def mod_of(batch, bk, ready):
                v.wait_ge(modt_ps, batch + 1)
                b_ = Sm("b_ada")[:, 16 * batch:16 * batch + 16].rearrange("p (c g) -> p c g", c=4)
                tt_(mod[:, 16 * batch:16 * batch + 16, :].rearrange("p (c g) s -> p c g s", c=4),
                    bank[bk].rearrange("p (c g r) -> p c g r", c=4, g=4)[:, :, :, 0:2],
                    b_.unsqueeze(3).broadcast_to([P, 4, 4, 2]), ALU.add).then_inc(ready, 1)

            def scaled(out, t0, g):
                return stt(out, mod[:, t0:t0 + KD, :], 1.0, Sm(g).unsqueeze(2).broadcast_to([P, KD, 2]), ALU.add, ALU.mult)

            mod_of(0, 3, mod1_ready)
            v.wait_ge(mod1_ready, 1)
            chain(scaled(s1, 8, "g1"))
            v.wait_ge(rstd1_ready, 1)
            for kk in range(KD):
                for cols, sq_ in SEQ:
                    stt(h[:, kk, cols], x[:, kk, cols], s1[:, kk, sq_:sq_ + 1], scr[:, 2, cols], ALU.mult, ALU.mult).then_inc(hs_ready, 1)

            for i in range(8):
                dst = q[:, i, :] if i < 4 else k[:, i - 4, 0:T]
                v.wait_ge(nrs_ready, i + 1)
                stt(dst, dst, gqs if i < 4 else Sm("gk"), scr[:, 2 + i % 2, 0:T], ALU.mult, ALU.mult).then_inc(qk_ready, 1)
            v.wait_ge(gates_ps, 1)
            cp(gtok[:, 0:2, :], bank[5][:, 0:16].rearrange("p (t g) -> p t g", t=2))
            cp(gtok[0:64, 2, :], bank[5][0:64, 16:24]).then_inc(gtok_ready, 1)
            for tt, (t0, n) in enumerate(TILES):
                v.wait_ge(vtr_ps, tt + 1)
                cp(vtok[0:n, tt, :], bank[2 + tt][0:n, :]).then_inc(vtok_ready, 1)
            v.wait_ge(grow_ps, 1)
            r4 = slice(0, MLH)
            chain.step(ts(rows[r4, 0, :], bank[6][r4, 0:T], Sm("bgate")[r4, 0:1], None, ALU.add))
            ts(rows[r4, 1, :], bank[7][r4, 0:T], Sm("bgate")[r4, 1:2], None, ALU.add).then_inc(frow_ready, 1)

            def gate_rows():
                v.wait_ge(flog_ready, 1)
                chain(stt(rows[r4, 1, :], rows[r4, 1, :], 0.0, rows[r4, 2, :], ALU.min, ALU.subtract))
                one = ones[r4, 0:1]
                for cols, sq_ in SEQ:
                    n = cols.stop - cols.start
                    chain.step(nc.vector.tensor_tensor_scan(rows[r4, 2, cols], one.broadcast_to([MLH, n]), rows[r4, 1, cols], 0.0, ALU.mult, ALU.add))
                chain.wait()
                chain(tt_(rows[r4, 0, :], rows[r4, 0, :], rows[r4, 2, :], ALU.subtract))
                for cols, sq_ in SEQ:
                    n = cols.stop - cols.start
                    chain.step(nc.vector.tensor_tensor_scan(rows[r4, 1, cols], one.broadcast_to([MLH, n]), rows[r4, 0, cols],
                                                            Sm("m0c")[r4, :] if sq_ else 0.0, ALU.mult, ALU.max))
                chain.wait()
                tt_(rows[r4, 3, :], rows[r4, 2, :], rows[r4, 1, :], ALU.add).then_inc(rows_ready, 1)

            def conv(j):
                wc = Sm("w_conv")[:, j * CW:(j + 1) * CW]
                v.wait_ge(proj_done, 5 + j)
                chain(ts(y[:, j, :], raw[:, j, 0:CONVW], wc[:, 0:1], Sm("b_conv")[:, j:j + 1], ALU.mult, ALU.add))
                for tap in range(1, CW):
                    ins = stt(y[:, j, :], raw[:, j, tap:tap + CONVW], wc[:, tap:tap + 1], y[:, j, :], ALU.mult, ALU.add)
                    if tap < CW - 1:
                        chain(ins)
                    else:
                        ins.then_inc(conv_ready, 1)

            for i in range(SBH + 2):
                if 1 <= i <= SBH:
                    v.wait_ge(between_ps, i)
                    t_ = scr[:, 3 * ((i - 1) % 2) + 2, :]
                    chain.wait()
                    tt_(t_, t_, bank[4 + (i - 1) % 2][:, :], ALU.subtract).then_inc(t_ready, 1)
                if i >= 3 and i % 2:
                    v.wait_ge(av_ps, i - 1)
                    cp(mix[:, (i - 3) // 2, :], bank[6][:, 0:T]).then_inc(av_done, 1)
                if i < SBH:
                    v.wait_ge(l_ready, i + 1)
                    b3 = 3 * (i % 2)
                    zb = bank[2 + i % 2][:, :]
                    stt(scr[:, b3 + 1, :], zb, 0.0, scr[:, b3, :], ALU.max, ALU.add).then_inc(sp_ready, 1)
                    if i >= 2:
                        v.wait_ge(av_ps, i - 1)
                    chain.step(stt(scr[:, b3 + 2, :], zb, 0.0, scr[:, b3, :], ALU.min, ALU.subtract))
                if 1 <= i <= 4:
                    conv(2 * i - 2)
                    conv(2 * i - 1)
                if i == 5:
                    gate_rows()

            v.wait_ge(sb_stored, 32)
            v.wait_ge(sgy_ready, 1)
            for cols, src in ((slice(0, TP), slice(0, TP)), (slice(TP, T), slice(CS, CONVW))):
                tt_(mq[:, :, cols], y[:, 0:4, src], sgy[:, 0:4, src], ALU.mult)
                stt(mk[:, :, cols], y[:, 4:8, src], MLD ** -0.5, sgy[:, 4:8, src], ALU.mult, ALU.mult)
            nc.vector.memset(mk[:, :, T:384], 0.0).then_inc(mkq_ready, 1)
            for tt, (t0, n) in enumerate(TILES):
                v.wait_ge(ktr_ps, tt + 1)
                cp(mktok[0:n, tt, :], bank[tt][0:n, :]).then_inc(ktok_ready, 1)
            v.wait_ge(acol_ps, 1)
            cp(acol[:, 0:2, :], bank[6][:, 0:8].rearrange("p (t h) -> p t h", t=2))
            cp(acol[0:64, 2, :], bank[6][0:64, 8:12]).then_inc(acol_ready, 1)
            v.wait_ge(acol_ready, 1)
            v.wait_ge(ld_state, 32)

            def ml_weights(i):
                Mb = bank[3]
                v.wait_ge(mb_ps, i + 1)
                ts(scr[:, 0, AC], Mb[:, 0:256], acol[:, 0, i:i + 1], 0.0, ALU.subtract, ALU.max)
                ts(scr[:, 0, B], Mb[:, 128:256], acol[:, 1, i:i + 1], 0.0, ALU.subtract, ALU.max)
                ts(scr[:, 0, E], Mb[:, 256:320], acol[:, 2, i:i + 1], 0.0, ALU.subtract, ALU.max).then_inc(wtmp_ready, 1)
                v.wait_ge(w_ready, i + 1)
                v.wait_ge(st_ps, i + 1)
                tt_(scr[:, 1, ACBE], bank[2][:, ACBE], scr[:, 0, ACBE], ALU.mult).then_inc(s_ready, 1)
                tt_(scr[:, 3, 0:64], mq[:, i, TP:T], scr[:, 3, 192:256], ALU.mult)
                ts(scr[:, 3, 64:192], ones, Sm("n0")[:, i:i + 1], None, ALU.mult).then_inc(qw_ready, 1)
                hc = slice(i * P, (i + 1) * P)
                ts(scr[:, 2, 0:128], mktok[:, 0, hc], scr[:, 0, 255:256], None, ALU.mult)
                ts(scr[:, 2, 128:256], mktok[:, 1, hc], scr[:, 0, 383:384], None, ALU.mult)
                ts(scr[0:64, 2, 256:384], mktok[0:64, 2, hc], scr[0:64, 0, 447:448], None, ALU.mult).then_inc(kw_ready, 1)

            def ml_out(i):
                v.wait_ge(hrs_ready, i + 1)
                chain(tt_(hh, hh, scr[:, 5, 0:T], ALU.mult))
                stt(mix[:, 4 + i, :], hh, Sm("gh"), mo_g[:, i, :], ALU.mult, ALU.mult).then_inc(mix_ready, 1)

            def ml_hidden(i):
                v.wait_ge(num_ps, i + 1)
                den = scr[:, 4, 0:T]
                chain(tt_(den, bank[6][:, 0:T], den, ALU.max))
                chain(stt(den, bank[6][:, 0:T], -1.0, den, ALU.mult, ALU.max))
                chain(nc.vector.reciprocal(den, den))
                tt_(hh, bank[5][:, 0:T], den, ALU.mult).then_inc(hd_ready, 1)
                v.wait_ge(hd_ready, i + 1)
                v.wait_ge(state_ps, i + 1)
                dec = scr[:, 3, 255:256]
                cp(Cout[:, 0, i, :], bank[1][:, 0:128])
                stt(Cout[:, 1, i, :], C0[:, i, :], dec, bank[1][:, 128:256], ALU.mult, ALU.add)
                cp(nout[:, 0, i:i + 1], bank[1][:, 256:257])
                stt(nout[:, 1, i:i + 1], Sm("n0")[:, i:i + 1], dec, bank[1][:, 257:258], ALU.mult, ALU.add).then_inc(state_out, 1)

            for i in range(MLH + 1):
                if i < MLH:
                    ml_weights(i)
                if i:
                    ml_out(i - 1)
                if i < MLH:
                    ml_hidden(i)
                if i == 1:
                    mod_of(1, 2, mod2_ready)

            mod_of(2, 2, mod2_ready)
            v.wait_ge(mod2_ready, 2)
            chain(scaled(s2, 32, "g2"))
            for t in range(8):
                v.wait_ge(xo_ps, t + 1)
                for cols, sq_ in SEQ:
                    stt(x[:, t, cols], bank[4 + t % 2][:, cols], mod[:, 16 + t, sq_:sq_ + 1], x[:, t, cols], ALU.mult, ALU.add).then_inc(x1_ready, 1)
            v.wait_ge(rstd2_ready, 1)
            v.wait_ge(x1_ready, 16)
            for kk in range(KD):
                for cols, sq_ in SEQ:
                    stt(h[:, kk, cols], x[:, kk, cols], s2[:, kk, sq_:sq_ + 1], scr[:, 2, cols], ALU.mult, ALU.mult).then_inc(hs2_ready, 1)

            nc.vector.memset(lg[64:128, 2, :], 0.0)
            v.wait_ge(logit_ps, 1)
            br = Sm("b_router")
            tt_(lg[:, 0:2, :], bank[6][:, 0:64].rearrange("p (t e) -> p t e", t=2), br.unsqueeze(1).broadcast_to([P, 2, NE]), ALU.add)
            chain(tt_(lg[0:64, 2, :], bank[6][0:64, 64:96], br[0:64, :], ALU.add))
            for tt in range(3):
                chain.step(nc.vector.max(top[:, tt, :], lg[:, tt, :]))
            chain.wait()
            for tt in range(3):
                chain.step(nc.vector.max_index(topi[:, tt, :], top[:, tt, :], lg[:, tt, :]))
            chain.wait()
            cp(topf, topi)
            ts(negv, top[:, :, 0], -1.0, None, ALU.mult).then_inc(top_ready, 1)
            v.wait_ge(top_ready, 1)
            for i in range(TOPK):
                for tt in range(3):
                    if i == 0:
                        chain.step(ts(member[:, tt, :], iota_e, topf[:, tt, 0:1], None, ALU.is_equal))
                    else:
                        chain.step(stt(member[:, tt, :], iota_e, topf[:, tt, i:i + 1], member[:, tt, :], ALU.is_equal, ALU.add))
                chain.wait()
            nc.vector.memset(member[64:128, 2, :], 0.0).then_inc(member_ready, 1)
            v.wait_ge(state_stored, 16 * 3)
            for i in range(6):
                tt, half = i // 2, i % 2
                n = TILES[tt][1]
                hc = slice(half * 512, half * 512 + 512)
                v.wait_ge(hi_ready, i + 1)
                tt_(res[0:n, i % 2, :], bank[i % 2][0:n, :], h2p[0:n, 0, tt, hc], ALU.subtract).then_inc(r_ready, 1)
                v.wait_ge(mid_ready, i + 1)
                tt_(h2p[0:n, 2, tt, hc], res[0:n, i % 2, :], h2p[0:n, 1, tt, hc], ALU.subtract).then_inc(lo_ready, 1)
            v.wait_ge(member_ready, 1)
            v.wait_ge(ex_ready, 3)
            chain(tt_(gate[:], gate[:], member[:], ALU.mult))
            chain(nc.vector.reduce_sum(rs4, gate[:], AX_X))
            chain(ts(rs4, rs4, 0.5, None, ALU.max))
            chain(nc.vector.reciprocal(rs4, rs4))
            chain(tt_(gate[:], gate[:], rs4.unsqueeze(2).broadcast_to([P, 3, NE]), ALU.mult))
            v.wait_ge(rank_ps, 1)
            chain(stt(rank[:], bank[5][:, 0:96].rearrange("p (t e) -> p t e", t=3), 1.0, member[:], ALU.add, ALU.mult))
            chain(ts(rank[:], rank[:], -1.0, None, ALU.add))
            chain(nc.vector.reduce_max(cmax, bank[5][:, 96:128], AX_X))
            cp(cnti, bank[5][:, 96:128])
            cp(cmaxi, cmax).then_inc(cnt_ready, 1)
            v.wait_ge(x1_ready, 16)
            nc.vector.memset(acc, 0.0).then_inc(acc_ready, 1)

            def picks(turn, e, groups):
                n = CAP // groups
                for tt, (t0, nt) in enumerate(TILES):
                    ts(pick[0:nt, tt, 0:n], iota_c[0:nt, 0:n], rank[0:nt, tt, bass.ds(e, 1)], None, ALU.is_equal).then_inc(pick_ready, 1)

            def wpicks(turn, e, groups):
                n = CAP // groups
                for tt, (t0, nt) in enumerate(TILES):
                    ts(wpick[0:nt, tt, :].rearrange("p (g n) -> p g n", g=groups),
                       iota_c[0:nt, 0:n].unsqueeze(1).broadcast_to([nt, groups, n]),
                       rank[0:nt, tt, bass.ds(e, 1)], gate[0:nt, tt, bass.ds(e, 1)],
                       ALU.is_equal, ALU.mult).then_inc(wpick_ready, 1)

            def bias_rows(e):
                ts(eh[0:NE, :], ones[0:NE, :], ident[0:NE, bass.ds(e, 1)], None, ALU.mult).then_inc(eh_ready, 1)

            def glu(i, turn, groups):
                v.wait_ge(gu_ps, turn * 2 + (i + 1))
                n = CHC // groups

                def two(t):
                    return t.rearrange("p (h n) -> p h n", h=2) if groups == 1 else t[:, 0:n]
                g_, l_ = (psum[:, 2:4, 0:256], psum[:, 2:4, 256:512]) if groups == 1 else (psum[:, 2 + i, 0:n], psum[:, 2 + i, n:2 * n])
                ts(two(gc), g_, SWIGLU_LIMIT, None, ALU.min).then_inc(gc_ready, 1)
                lc_ = lc[:, i, :]
                ts(two(lc_), l_, SWIGLU_LIMIT, -SWIGLU_LIMIT, ALU.min, ALU.max).then_inc(lc_ready, 1)
                v.wait_ge(lc_ready, turn * 2 + (i + 1))
                stt(lc_[:, 0:n], lc_[:, 0:n], 1.0, gc[:, 0:n], ALU.add, ALU.mult).then_inc(gl_ready, 1)
                v.wait_ge(gl_ready, turn * 2 + (i + 1))
                v.wait_ge(sg_ready, turn * 2 + (i + 1))
                tt_(act[:, i, 0:n], lc_[:, 0:n], sg[:, 0:n], ALU.mult).then_inc(act_ready, 1)

            def add(i, turn):
                if i == 0:
                    v.wait_ge(acc_ready, turn * 8 + 1)
                for c in range(2):
                    for hf in range(2):
                        v.wait_ge(sc_ps, turn * 8 + (4 * i + 2 * c + hf + 1))
                        t_ = acc[:, 4 * i + 2 * hf + c, :]
                        tt_(t_, bank[4 + 2 * c + hf][:, 0:T], t_, ALU.add).then_inc(acc_ready, 1)

            def start(turn, e, b):
                n = count(v, e)
                if not isinstance(b, int):
                    ts(rank[:], rank[:], float(-CAP), None, ALU.add).then_inc(rank_moved, 1)
                    v.wait_ge(rank_moved, b)
                bias_rows(e)
                by_size(v, n, b, lambda groups: picks(turn, e, groups))

            def expert(turn, e, b, begins, ends):
                n = count(v, e)
                after = None if ends else count(v, e + 1)
                by_size(v, n, b, lambda groups: glu(0, turn, groups))
                if not ends:
                    by_size(v, after, b, lambda groups: picks(turn + 1, e + 1, groups))
                if not begins:
                    add(0, turn - 1)
                by_size(v, n, b, lambda groups: (glu(1, turn, groups), wpicks(turn, e, groups)))
                if not begins:
                    add(1, turn - 1)
                v.wait_ge(dn_ps, turn * 2 + 2)
                if not ends:
                    bias_rows(e + 1)

            def finish(turn, b):
                add(0, turn)
                add(1, turn)

            passes(v, start, expert, finish)
            nc.vector.memset(cmax, 0.0).then_inc(acc_closed, 1)
            v.wait_ge(acc_closed, 1)
            for kk in range(KD):
                for cols, sq_ in SEQ:
                    stt(h[:, kk, cols], acc[:, kk, cols], mod[:, 40 + kk, sq_:sq_ + 1], x[:, kk, cols], ALU.mult, ALU.add).then_inc(y_ready, 1)

        @block.gpsimd
        def _(g):
            g.wait_ge(ld_small, 64)

            def masked(buf, mask, ready):
                nc.gpsimd.tensor_tensor(scr[:, buf, A], scr[:, buf, A], mask[:, A], ALU.mult)
                nc.gpsimd.tensor_tensor(scr[:, buf, BE], scr[:, buf, BE], mask[:, BE], ALU.mult).then_inc(ready, 1)

            for i in range(SBH + 1):
                if i:
                    g.wait_ge(e_ready, i)
                    masked(3 * ((i - 1) % 2) + 2, mask_s, a_ready)
                if i < SBH:
                    g.wait_ge(sp_ready, i + 1)
                    masked(3 * (i % 2) + 1, mask_s, spm_ready)
            for i in range(MLH):
                g.wait_ge(s_ready, i + 1)
                masked(1, mask_i, sm_ready)


_OUTS = (("yT", (D, T)), ("koT", (512, T)), ("voT", (512, T)), ("convo", (D, 2, 3)), ("co", (2, MLH, P, P)),
         ("no", (P, 2 * MLH)), ("mo", (MLH, 2)))


def constants():
    c = np.zeros((P, NCONST), np.float32)

    def put(name, a):
        c[:a.shape[0], CONST[name][0]:CONST[name][0] + a.shape[1]] = a
    i = np.arange(P)
    put("ident", np.eye(P, dtype=np.float32))
    put("ones", np.ones((P, P), np.float32))
    put("tri", (i[:, None] > i[None, :]).astype(np.float32))
    put("blk", (i[:, None] // SBD == i[None, :] // SBD).astype(np.float32))
    for name, before in (("mask_s", i[:, None] < i[None, :]), ("mask_i", i[:, None] <= i[None, :])):
        m = np.zeros((P, 448), np.float32)
        m[:, A] = before
        m[:, C] = 1
        m[:, B] = before
        m[:64, E] = before[:64, :64]
        put(name, m)
    sel = np.zeros((MLH, MLH, P), np.float32)
    for j in range(MLH):
        sel[j, j] = 1
    put("sel", sel.reshape(MLH, MLH * P))
    put("iota", np.tile(np.arange(CAP, dtype=np.float32), (P, 1)))
    return c


def kernel(x_prompt, x_sample, c_prompt, c_sample, cache_sb_k, cache_sb_v, state_conv, state_mlstm_c,
           state_mlstm_n, state_mlstm_m, w_ada, b_ada, g_norm1, w_in, g_q, g_k, w_conv, b_conv, b_gate,
           g_head, w_out, g_norm2, w_router, b_router, w_gu, b_gu, w_down, b_down):
    import concourse.bacc as bacc
    from concourse.bass_utils import run_bass_kernel_spmd

    def A_(a):
        return np.asarray(a)

    small = np.zeros((P, NSMALL), np.float32)

    def put(name, a):
        a = np.asarray(a)
        small[:a.shape[0], SMALL[name][0]:SMALL[name][0] + a.shape[1]] = a

    put("g1", A_(g_norm1)[0].reshape(KD, P).T)
    put("g2", A_(g_norm2)[0].reshape(KD, P).T)
    put("b_ada", A_(b_ada)[0].reshape(48, P).T)
    put("b_conv", A_(b_conv)[0].reshape(8, P).T)
    put("w_conv", A_(w_conv)[0].reshape(CW, 8, P).transpose(2, 1, 0).reshape(P, 8 * CW))
    put("gq", np.tile(A_(g_q)[0], 2)[:, None])
    put("gk", np.tile(A_(g_k)[0], 2)[:, None])
    put("gh", A_(g_head)[0][:, None])
    put("n0", A_(state_mlstm_n)[0, 0].T)
    put("cT", np.stack([A_(c_prompt)[0].reshape(KD, P), A_(c_sample)[0].reshape(KD, P)], -1).transpose(1, 0, 2).reshape(P, 16))
    put("m0b", np.tile(A_(state_mlstm_m)[0, 0][None, :], (P, 1)))
    put("m0c", A_(state_mlstm_m)[0, 0][:, None])
    put("b_router", np.tile(A_(b_router)[0][None, :], (P, 1)))
    put("eps", np.full((P, 1), 1e-6, np.float32))
    put("conv_past", A_(state_conv)[0, 0].reshape(3, 8, P).transpose(2, 1, 0).reshape(P, 24))
    put("bgate", A_(b_gate)[0].reshape(2, MLH).T)
    put("w_router", A_(w_router)[0].reshape(KD, P, NE).transpose(1, 0, 2).reshape(P, KD * NE))
    c0_ = A_(state_mlstm_c)[0, 0]
    arrays = {
        "xT": np.concatenate([A_(x_prompt)[0], A_(x_sample)[0]], 0).T,
        "small": small,
        "const": constants(),
        "b_exp": np.concatenate([A_(b_gu)[0], A_(b_down)[0]], 1),
        "kcT": A_(cache_sb_k)[0, 0].reshape(PAST, 512).T,
        "vc": A_(cache_sb_v)[0, 0].reshape(PAST, 512),
        "c0": c0_.transpose(1, 0, 2),
        "c0T": c0_.transpose(2, 0, 1),
        "w_ada": A_(w_ada), "w_in": A_(w_in), "w_out": A_(w_out), "w_gu": A_(w_gu), "w_down": A_(w_down),
    }
    arrays = {n: np.ascontiguousarray(a) for n, a in arrays.items()}
    nc = bacc.Bacc("TRN2", target_bir_lowering=False, num_devices=1)
    args = [nc.dram_tensor(n, a.shape, mybir.dt.from_np(a.dtype), kind="ExternalInput").ap() for n, a in arrays.items()]
    args += [nc.dram_tensor(n, shape, F32, kind="ExternalOutput").ap() for n, shape in _OUTS]
    build(nc, *args)
    r = run_bass_kernel_spmd(nc, [arrays], core_ids=[0]).results[0]
    y = np.ascontiguousarray(r["yT"].T)
    kk = np.ascontiguousarray(r["koT"].T).reshape(T, SBH, SBD)
    vv = np.ascontiguousarray(r["voT"].T).reshape(T, SBH, SBD)
    cv = r["convo"].transpose(1, 2, 0)
    n = r["no"].reshape(P, 2, MLH).transpose(1, 2, 0)
    m = r["mo"].T

    def out(a):
        return np.ascontiguousarray(a)[None, None]
    return (y[None, :TP], y[None, TP:], out(kk[:TP]), out(vv[:TP]), out(cv[0]), out(r["co"][0]), out(n[0]), out(m[0]),
            out(kk[TP:]), out(vv[TP:]), out(cv[1]), out(r["co"][1]), out(n[1]), out(m[1]))
```
